# Optimizing a Trainium2 kernel written in Bass

```python
import math
import jax, jax.numpy as jnp
from jax import lax
import numpy as np

D_MODEL = 1024
BATCH = 1
SEQ = 256
DEPTH = 2

CHUNK = 64
N_Q_HEADS = 8
N_KV_HEADS = 2
HEAD_DIM = 64
Q_GROUP = N_Q_HEADS // N_KV_HEADS
WINDOW = 128
WINDOW_CHUNKS = WINDOW // CHUNK
ROT_DIM = HEAD_DIM // 4
ROPE_THETA = 500000.0
ATTN_Q_WIDTH = N_Q_HEADS * HEAD_DIM
ATTN_KV_WIDTH = N_KV_HEADS * HEAD_DIM
GMLP_GROUPS = 4
GMLP_SPAN = 128
GMLP_WIDTH = 512
GMLP_GROUP_DIM = GMLP_WIDTH // GMLP_GROUPS
IN_WIDTH = ATTN_Q_WIDTH + 2 * ATTN_KV_WIDTH + 2 * GMLP_WIDTH + 2 * D_MODEL
SPLIT_POINTS = (
    ATTN_Q_WIDTH,
    ATTN_Q_WIDTH + ATTN_KV_WIDTH,
    ATTN_Q_WIDTH + 2 * ATTN_KV_WIDTH,
    ATTN_Q_WIDTH + 2 * ATTN_KV_WIDTH + 2 * GMLP_WIDTH,
    ATTN_Q_WIDTH + 2 * ATTN_KV_WIDTH + 2 * GMLP_WIDTH + D_MODEL,
)
PEER_HEADS = 8
PEER_N_KEYS = 128
PEER_N_EXPERTS = PEER_N_KEYS * PEER_N_KEYS
PEER_KEY_DIM = 256
PEER_HALF = PEER_KEY_DIM // 2
PEER_TOPK = 16
PEER_TOKEN_BLOCK = 128

NORM_EPS = 1e-6
MASK_VALUE = -1e30

kernel_name = "hybrid_swa_sink_gmlp_peer_trunk"

def rms_norm(x, g):
    xf = x.astype(jnp.float32)
    y = xf * lax.rsqrt(jnp.mean(xf * xf, axis=-1, keepdims=True) + NORM_EPS)
    return y.astype(x.dtype) * g

def layer_norm(x, g, b):
    xf = x.astype(jnp.float32)
    mu = jnp.mean(xf, axis=-1, keepdims=True)
    var = jnp.mean(jnp.square(xf - mu), axis=-1, keepdims=True)
    y = (xf - mu) * lax.rsqrt(var + NORM_EPS)
    return y.astype(x.dtype) * g + b

def partial_rope(t, positions):
    half = ROT_DIM // 2
    inv_freq = ROPE_THETA ** (-jnp.arange(half, dtype=jnp.float32) / half)
    ang = positions.astype(jnp.float32)[..., None] * inv_freq
    cos = jnp.cos(ang)[:, :, None, :].astype(t.dtype)
    sin = jnp.sin(ang)[:, :, None, :].astype(t.dtype)
    t1, t2, rest = t[..., :half], t[..., half:ROT_DIM], t[..., ROT_DIM:]
    return jnp.concatenate([t1 * cos - t2 * sin, t2 * cos + t1 * sin, rest], axis=-1)

def sliding_window_attention(q, k, v, sinks):
    B, S = q.shape[0], q.shape[1]
    n_chunks = S // CHUNK
    qc = q.reshape(B, n_chunks, CHUNK, N_KV_HEADS, Q_GROUP, HEAD_DIM)
    kc = k.reshape(B, n_chunks, CHUNK, N_KV_HEADS, HEAD_DIM)
    vc = v.reshape(B, n_chunks, CHUNK, N_KV_HEADS, HEAD_DIM)
    pad = ((0, 0), (WINDOW_CHUNKS - 1, 0), (0, 0), (0, 0), (0, 0))
    kp, vp = jnp.pad(kc, pad), jnp.pad(vc, pad)
    k_band = jnp.concatenate([kp[:, i:i + n_chunks] for i in range(WINDOW_CHUNKS)], axis=2)
    v_band = jnp.concatenate([vp[:, i:i + n_chunks] for i in range(WINDOW_CHUNKS)], axis=2)
    s = jnp.einsum('bcqhgd,bckhd->bhgcqk', qc, k_band).astype(jnp.float32) * (HEAD_DIM ** -0.5)
    chunk_off = jnp.arange(WINDOW_CHUNKS * CHUNK) // CHUNK - (WINDOW_CHUNKS - 1)
    valid = (jnp.arange(n_chunks)[:, None] + chunk_off[None, :]) >= 0
    s = jnp.where(valid[None, None, None, :, None, :], s, MASK_VALUE)
    sink = sinks.astype(jnp.float32).reshape(N_KV_HEADS, Q_GROUP)[None, :, :, None, None, None]
    m = jnp.maximum(jnp.max(s, axis=-1, keepdims=True), sink)
    p = jnp.exp(s - m)
    p = p / (jnp.sum(p, axis=-1, keepdims=True) + jnp.exp(sink - m))
    o = jnp.einsum('bhgcqk,bckhd->bcqhgd', p.astype(v.dtype), v_band)
    return o.reshape(B, S, ATTN_Q_WIDTH)

def gmlp_spatial_gating(z, ln_g, ln_b, w_s, b_s):
    B, S = z.shape[0], z.shape[1]
    z = jax.nn.gelu(z, approximate=False)
    u, v = jnp.split(z, 2, axis=-1)
    v = layer_norm(v, ln_g, ln_b)
    n_groups = S // GMLP_SPAN
    vb = v.reshape(B, n_groups, GMLP_SPAN, GMLP_GROUPS, GMLP_GROUP_DIM)
    pos_chunk = jnp.arange(GMLP_SPAN) // CHUNK
    mask = pos_chunk[None, :] <= pos_chunk[:, None]
    w = jnp.where(mask[None], w_s, 0.0)
    s = jnp.einsum('gij,bnjgc->bnigc', w.astype(v.dtype), vb) + b_s.T[None, None, :, :, None]
    return u * s.reshape(B, S, GMLP_WIDTH)

def peer(xn, w_query, sub_keys, u_tab, v_tab):
    B, S, D = xn.shape
    q = (xn @ w_query).reshape(B, S, PEER_HEADS, PEER_KEY_DIM)
    q1, q2 = q[..., :PEER_HALF], q[..., PEER_HALF:]
    s1 = jnp.einsum('bshd,hkd->bshk', q1, sub_keys[:, 0]).astype(jnp.float32)
    s2 = jnp.einsum('bshd,hkd->bshk', q2, sub_keys[:, 1]).astype(jnp.float32)
    v1, i1 = lax.top_k(s1, PEER_TOPK)
    v2, i2 = lax.top_k(s2, PEER_TOPK)
    cand = (v1[..., :, None] + v2[..., None, :]).reshape(B, S, PEER_HEADS, PEER_TOPK * PEER_TOPK)
    sc, idx = lax.top_k(cand, PEER_TOPK)
    ia = jnp.take_along_axis(i1, idx // PEER_TOPK, axis=-1)
    ib = jnp.take_along_axis(i2, idx % PEER_TOPK, axis=-1)
    experts = ia * PEER_N_KEYS + ib
    gates = jax.nn.softmax(sc, axis=-1).astype(xn.dtype)
    n_blocks = (B * S) // PEER_TOKEN_BLOCK
    xb = xn.reshape(n_blocks, PEER_TOKEN_BLOCK, D)
    eb = experts.reshape(n_blocks, PEER_TOKEN_BLOCK, PEER_HEADS * PEER_TOPK)
    gb = gates.reshape(n_blocks, PEER_TOKEN_BLOCK, PEER_HEADS * PEER_TOPK)

    def block(args):
        xt, et, gt = args
        u = jnp.take(u_tab, et, axis=0)
        h = jax.nn.gelu(jnp.einsum('td,tkd->tk', xt, u), approximate=False)
        v = jnp.take(v_tab, et, axis=0)
        return jnp.einsum('tk,tkd->td', gt * h, v)

    out = lax.map(block, (xb, eb, gb))
    return out.reshape(B, S, D)

def setup_inputs(seed: int = 0) -> dict:
    key = jax.random.key(seed)
    ks = jax.random.split(key, 20)
    f32 = jnp.float32
    nrm = lambda k, shape, scale: jax.random.normal(k, shape, f32) * scale
    x = jax.random.normal(ks[0], (BATCH, SEQ, D_MODEL), f32)
    offsets = jax.random.randint(ks[1], (BATCH, 1), 0, 128, dtype=jnp.int32) * CHUNK
    positions = (offsets + jnp.arange(SEQ, dtype=jnp.int32)[None, :]).astype(jnp.int32)
    return {
        "x": x,
        "positions": positions,
        "norm_mix_g": 1.0 + nrm(ks[2], (DEPTH, D_MODEL), 0.02),
        "w_in": nrm(ks[3], (DEPTH, D_MODEL, IN_WIDTH), D_MODEL ** -0.5),
        "attn_sinks": nrm(ks[4], (DEPTH, N_Q_HEADS), 0.5),
        "gmlp_ln_g": 1.0 + nrm(ks[5], (DEPTH, GMLP_WIDTH), 0.02),
        "gmlp_ln_b": nrm(ks[6], (DEPTH, GMLP_WIDTH), 0.02),
        "w_spatial": nrm(ks[7], (DEPTH, GMLP_GROUPS, GMLP_SPAN, GMLP_SPAN), 0.5 * GMLP_SPAN ** -0.5),
        "b_spatial": 1.0 + nrm(ks[8], (DEPTH, GMLP_GROUPS, GMLP_SPAN), 0.1),
        "w_attn_branch": nrm(ks[9], (DEPTH, ATTN_Q_WIDTH, D_MODEL), ATTN_Q_WIDTH ** -0.5),
        "w_gmlp_branch": nrm(ks[10], (DEPTH, GMLP_WIDTH, D_MODEL), GMLP_WIDTH ** -0.5),
        "w_out": nrm(ks[11], (DEPTH, D_MODEL, D_MODEL), D_MODEL ** -0.5),
        "norm_ffn_g": 1.0 + nrm(ks[12], (DEPTH, D_MODEL), 0.02),
        "peer_w_query": nrm(ks[13], (DEPTH, D_MODEL, PEER_HEADS * PEER_KEY_DIM), D_MODEL ** -0.5),
        "peer_sub_keys": nrm(ks[14], (DEPTH, PEER_HEADS, 2, PEER_N_KEYS, PEER_HALF), PEER_HALF ** -0.5),
        "peer_u": nrm(ks[15], (DEPTH, PEER_N_EXPERTS, D_MODEL), D_MODEL ** -0.5),
        "peer_v": nrm(ks[16], (DEPTH, PEER_N_EXPERTS, D_MODEL), 0.1),
        "final_norm_g": 1.0 + nrm(ks[17], (D_MODEL,), 0.02),
    }

def reference(x, positions, norm_mix_g, w_in, attn_sinks, gmlp_ln_g, gmlp_ln_b, w_spatial,
              b_spatial, w_attn_branch, w_gmlp_branch, w_out, norm_ffn_g, peer_w_query,
              peer_sub_keys, peer_u, peer_v, final_norm_g):
    B, S = x.shape[0], x.shape[1]
    h = x
    for l in range(DEPTH):
        xn = rms_norm(h, norm_mix_g[l])
        z = xn @ w_in[l]
        q, k, v, z_gmlp, g_a, g_b = jnp.split(z, SPLIT_POINTS, axis=-1)
        q = partial_rope(q.reshape(B, S, N_Q_HEADS, HEAD_DIM), positions)
        k = partial_rope(k.reshape(B, S, N_KV_HEADS, HEAD_DIM), positions)
        v = v.reshape(B, S, N_KV_HEADS, HEAD_DIM)
        attn = sliding_window_attention(q, k, v, attn_sinks[l])
        spat = gmlp_spatial_gating(z_gmlp, gmlp_ln_g[l], gmlp_ln_b[l], w_spatial[l], b_spatial[l])
        merged = (jax.nn.sigmoid(g_a) * (attn @ w_attn_branch[l])
                  + jax.nn.sigmoid(g_b) * (spat @ w_gmlp_branch[l]))
        h = h + merged @ w_out[l]
        h = h + peer(rms_norm(h, norm_ffn_g[l]), peer_w_query[l], peer_sub_keys[l], peer_u[l], peer_v[l])
    return rms_norm(h, final_norm_g)


_drawn_inputs = setup_inputs


def setup_inputs(seed=0):
    import zlib

    import numpy as np

    out = dict(_drawn_inputs(seed))
    spreads = {}
    factors = {'norm_mix_g': 3.74,
     'attn_sinks': 64.0,
     'gmlp_ln_g': 8.0,
     'gmlp_ln_b': 8.0,
     'norm_ffn_g': 21.702,
     'final_norm_g': 8.244}
    for name, (base, spread) in spreads.items():
        noise = np.random.default_rng([zlib.crc32(name.encode()), seed]).standard_normal(out[name].shape)
        drawn = base * np.exp(spread * noise) if base else spread * noise
        out[name] = __import__('jax').numpy.asarray(drawn.astype(out[name].dtype))
    for name, factor in factors.items():
        out[name] = (out[name] * factor).astype(out[name].dtype)
    return out
```

```python
from contextlib import ExitStack

import numpy as np

import concourse.bass as bass
from concourse import mybir

F32 = mybir.dt.float32
I32 = mybir.dt.int32
U32 = mybir.dt.uint32
ALU = mybir.AluOpType
ACT = mybir.ActivationFunctionType
AX = mybir.AxisListType.X

P = 128
BLOCKS = 2
DM = 1024
KT = DM // P
DEPTH = 2
STEPS = DEPTH * BLOCKS
CH = 64
NH, NKV, HD = 8, 2, 64
GRP = NH // NKV
ROT = HD // 4
HALF = ROT // 2
THETA = 500000.0
GW, GG = 512, 4
GD = GW // GG
PH, NK, KD = 8, 128, 128
SIDES = 2 * PH
NE = NK * NK
TOPK = 16
PICKS = PH * TOPK
EPS = 1e-6
MASKED = -1e30
LOWEST = -3.0e38
BANK = 512

UNIT = 8
UNITS = PICKS // UNIT
LAG = 2
RING = 4
TURNS = UNIT // RING
WSLOTS = 3

PI_DOWN = float(np.nextafter(np.float32(np.pi), np.float32(0)))
ROUND = float(1.5 * 2 ** 23)


def two_pi_parts():
    rest, parts = 2 * np.pi, []
    for _ in range(3):
        scale = 2.0 ** (np.floor(np.log2(rest)) - 7)
        parts.append(float(np.floor(rest / scale) * scale))
        rest -= parts[-1]
    return parts + [float(rest)]


IN_COLS = [(0, 512), (512, 256), (768, 512), (1280, 512), (1792, 512), (2304, 512), (2816, 512), (3328, 512)]
Q, KV, ZU, ZV, GA0, GA1, GB0, GB1, W_ATTN, W_GMLP, W_OUT0, W_OUT1, W_QRY0 = range(13)
CHUNKS = 16


def chunk_number(d, c):
    layer, block = divmod(d, BLOCKS)
    before = d * CHUNKS + layer + block
    if c == "keys":
        return before + W_QRY0
    return before + c + (1 if block == 0 and c >= W_QRY0 else 0)


def build(nc, x, positions, norm_mix_g, w_in, attn_sinks, gmlp_ln_g, gmlp_ln_b, w_spatial, b_spatial,
          w_attn_branch, w_gmlp_branch, w_out, norm_ffn_g, peer_w_query, peer_sub_keys, peer_u, peer_v,
          final_norm_g, out):
    u_rows = peer_u.rearrange("l e d -> (l e) d")
    v_rows = peer_v.rearrange("l e d -> (l e) d")

    with ExitStack() as ctx:
        def sb(name, shape, dt=F32):
            return ctx.enter_context(nc.sbuf_tensor(name, shape, dt))

        def sem(name):
            return ctx.enter_context(nc.semaphore(name))

        h = [sb(f"h{b}", [P, DM]) for b in range(BLOCKS)]
        xf = [sb(f"xf{b}", [P, DM]) for b in range(BLOCKS)]
        xm = sb("xm", [P, DM])
        xT = sb("xT", [P, KT, P])
        qk = sb("qk", [P, 5, 2, HD])
        v_tok = [sb(f"v_tok{b}", [P, NKV, HD]) for b in range(BLOCKS)]
        qT = sb("qT", [P, GRP, P])
        kT = [sb(f"kT{b}", [P, P]) for b in range(BLOCKS)]
        gu = sb("gu", [P, GW])
        gv = sb("gv", [P, GW])
        sig = sb("sig", [P, 2, DM])
        probs = sb("probs", [P, NH, 2, P])
        side_scores = probs[:, :, :, :].rearrange("p h s k -> p (h s) k")
        turned = sb("turned", [P, SIDES, P])
        attn = sb("attn", [P, NH, HD])
        spat = sb("spat", [P, GW])
        attnT = sb("attnT", [P, 4, P])
        spatT = sb("spatT", [P, 4, P])
        rt = sb("rt", [P, 4, 10, HALF])
        keysT = sb("keysT", [P, SIDES, NK])
        w_sp = sb("w_sp", [P, GG, P])
        w_spT = sb("w_spT", [P, GG, P])
        gain_mix = sb("gain_mix", [P, DM])
        gain_ffn = sb("gain_ffn", [P, DM])
        ln_g = sb("ln_g", [P, GW])
        ln_b = sb("ln_b", [P, GW])
        b_sp = sb("b_sp", [P, DEPTH, GG])
        sinks = sb("sinks", [P, DEPTH, NH])
        mask = sb("mask", [P, 2, P])
        ident = sb("ident", [P, P])
        pos = sb("pos", [P, BLOCKS], I32)
        inv_freq = sb("inv_freq", [P, HALF])
        ang = sb("ang", [P, BLOCKS, HALF])
        turn_n = sb("turn_n", [P, BLOCKS, HALF])
        cos = sb("cos", [P, BLOCKS, HALF])
        sin = sb("sin", [P, BLOCKS, HALF])
        iota = sb("iota", [P, TOPK])
        stat = sb("stat", [P, 8])
        att_m = sb("att_m", [P, 4, NH])
        top_v = sb("top_v", [P, SIDES, TOPK])
        top_i = sb("top_i", [P, SIDES, TOPK], U32)
        cand = sb("cand", [P, 2, TOPK, TOPK])
        pair_s = sb("pair_s", [P, PH, TOPK])
        pair_i = sb("pair_i", [P, PICKS], U32)
        pair_ab = sb("pair_ab", [P, 2, PICKS], U32)
        key_ab = sb("key_ab", [P, 3, PICKS])
        gsum = sb("gsum", [P, PH])
        gates = [sb(f"gates{b}", [P, PICKS]) for b in range(BLOCKS)]
        ids = [sb(f"ids{b}", [P, PICKS], I32) for b in range(BLOCKS)]
        dots = sb("dots", [P, PICKS])
        acts = sb("acts", [P, PICKS])
        coef = sb("coef", [P, PICKS])
        junk = sb("junk", [P, DM])
        staged = sb("staged", [P, 2, 2, UNIT], I32)
        u_ring = sb("u_ring", [P, RING, DM])
        v_ring = sb("v_ring", [P, RING, DM])
        w_ring = sb("w_ring", [P, WSLOTS, KT * BANK])
        ps = ctx.enter_context(nc.psum_tensor("ps", [P, 8 * BANK], F32))

        def bank(n, width=BANK):
            return ps[:, n * BANK:n * BANK + width]

        x_in = sem("x_in")
        gains_in = sem("gains_in")
        final_in = sem("final_in")
        w_landed = [sem(f"w_landed{s}") for s in range(WSLOTS)]
        w_used = sem("w_used")
        out_done = sem("out_done")
        consts = sem("consts")
        rope_args = sem("rope_args")
        rope_tab = sem("rope_tab")
        dve = sem("dve")
        sq_in = sem("sq_in")
        sq_out = sem("sq_out")
        xm_ready = sem("xm_ready")
        xmT_ps = sem("xmT_ps")
        xmT_ready = sem("xmT_ready")
        w_spT_ps = sem("w_spT_ps")
        w_spT_ready = sem("w_spT_ready")
        in_out = sem("in_out")
        roped = sem("roped")
        qkT_ps = sem("qkT_ps")
        qkT_ready = sem("qkT_ready")
        att_ps = sem("att_ps")
        att_max = sem("att_max")
        att_exp = sem("att_exp")
        probsT_ps = sem("probsT_ps")
        probsT_ready = sem("probsT_ready")
        pv_ps = sem("pv_ps")
        attn_ready = sem("attn_ready")
        ln_ready = sem("ln_ready")
        spat_ps = sem("spat_ps")
        spat_ready = sem("spat_ready")
        branchT_ps = sem("branchT_ps")
        branchT_ready = sem("branchT_ready")
        merged = sem("merged")
        mergedT_ps = sem("mergedT_ps")
        mergedT_ready = sem("mergedT_ready")
        xf_ready = sem("xf_ready")
        xfT_ps = sem("xfT_ps")
        xfT_ready = sem("xfT_ready")
        keysT_ready = sem("keysT_ready")
        qry_ready = sem("qry_ready")
        side_ps = sem("side_ps")
        side_ready = sem("side_ready")
        gate_args = sem("gate_args")
        gate_exp = sem("gate_exp")
        routed = sem("routed")
        staged_sem = sem("staged")
        u_landed = [sem(f"u_landed{s}") for s in range(RING)]
        v_landed = [sem(f"v_landed{s}") for s in range(RING)]
        u_used = sem("u_used")
        v_used = sem("v_used")
        gelu_done = sem("gelu_done")
        coef_ready = sem("coef_ready")
        y_ready = sem("y_ready")

        block_ctx = ctx.enter_context(nc.Block())

        @block_ctx.sync
        def _(sp):
            def load_layer(l):
                sp.dma_start(gain_mix[:, :], norm_mix_g[l, :].partition_broadcast(P)).then_inc(gains_in, 16)
                sp.dma_start(w_sp[:, :, :], w_spatial[l].rearrange("g i j -> i g j")).then_inc(gains_in, 16)
                sp.dma_start(ln_g[:, :], gmlp_ln_g[l, :].partition_broadcast(P)).then_inc(gains_in, 16)
                sp.dma_start(ln_b[:, :], gmlp_ln_b[l, :].partition_broadcast(P)).then_inc(gains_in, 16)
                sp.dma_start(gain_ffn[:, :], norm_ffn_g[l, :].partition_broadcast(P)).then_inc(gains_in, 16)

            def load_chunk(n, dst, src):
                if n >= WSLOTS:
                    sp.wait_ge(w_used, n - WSLOTS + 1)
                sp.dma_start(dst, src).then_inc(w_landed[n % WSLOTS], 16)

            def load_weights(d, first, last):
                l, b = divmod(d, BLOCKS)
                for c in range(first, last):
                    n = chunk_number(d, c)
                    slot = w_ring[:, n % WSLOTS, :]
                    if c <= GB1:
                        c0, cols = IN_COLS[c]
                        load_chunk(n, slot[:, 0:KT * cols].rearrange("p (k n) -> p k n", k=KT),
                                   w_in[l, :, c0:c0 + cols].rearrange("(k p) n -> p k n", p=P))
                    elif c in (W_ATTN, W_GMLP):
                        w = w_attn_branch if c == W_ATTN else w_gmlp_branch
                        load_chunk(n, slot.rearrange("p (k n) -> p k n", k=4),
                                   w[l].rearrange("(k p) n -> p k n", p=P))
                    elif c in (W_OUT0, W_OUT1):
                        c0 = (c - W_OUT0) * BANK
                        load_chunk(n, slot.rearrange("p (k n) -> p k n", k=KT),
                                   w_out[l, :, c0:c0 + BANK].rearrange("(k p) n -> p k n", p=P))
                    else:
                        if c == W_QRY0 and b == 0:
                            n0 = chunk_number(d, "keys")
                            load_chunk(n0, w_ring[:, n0 % WSLOTS, 0:SIDES * KD].rearrange("p (s d) -> p s d", s=SIDES),
                                       peer_sub_keys[l].rearrange("h t k d -> k (h t) d"))
                        c0 = (c - W_QRY0) * BANK
                        load_chunk(n, slot.rearrange("p (k n) -> p k n", k=KT),
                                   peer_w_query[l, :, c0:c0 + BANK].rearrange("(k p) n -> p k n", p=P))

            sp.dma_start(h[0][:, :], x[0, 0:P, :]).then_inc(x_in, 16)
            sp.dma_start(pos[:, :], positions[0].rearrange("(b p) -> p b", p=P),
                         allow_slow_non_contiguous=True).then_inc(x_in, 16)
            load_weights(0, Q, KV)
            load_layer(0)
            sp.dma_start(h[1][:, :], x[0, P:2 * P, :]).then_inc(x_in, 16)
            sp.dma_start(sinks[:, :, :], attn_sinks.partition_broadcast(P)).then_inc(x_in, 16)
            for l in range(DEPTH):
                sp.dma_start(b_sp[:, l, :], b_spatial[l].rearrange("g i -> i g"),
                             allow_slow_non_contiguous=True).then_inc(x_in, 16)
            load_weights(0, KV, CHUNKS)
            load_weights(1, Q, CHUNKS)
            sp.wait_ge(xf_ready, 2)
            load_layer(1)
            load_weights(2, Q, CHUNKS)
            load_weights(3, Q, CHUNKS)
            sp.wait_ge(xm_ready, 4)
            sp.dma_start(gain_mix[:, :], final_norm_g.partition_broadcast(P)).then_inc(final_in, 16)
            for b in range(BLOCKS):
                sp.wait_ge(y_ready, b + 1)
                sp.dma_start(out[0, b * P:(b + 1) * P, :], xf[b][:, :]).then_inc(out_done, 16)
            sp.wait_ge(out_done, 16 * BLOCKS)

        @block_ctx.gpsimd
        def _(pool):
            pool.memset(ident[:, :], 0.0).then_inc(consts, 1)
            pool.memset(mask[:, :, :], 0.0).then_inc(consts, 1)
            pool.iota(iota[:, :], [[1, TOPK]], base=0, channel_multiplier=0,
                      allow_small_or_imprecise_dtypes=True).then_inc(consts, 1)
            pool.wait_ge(consts, 3)
            pool.affine_select(out=ident[:, :], in_=ident[:, :], compare_op=ALU.not_equal, fill=1.0, base=0,
                               pattern=[[-1, P]], channel_multiplier=1).then_inc(consts, 1)
            pool.memset(mask[:, 0, 0:CH], MASKED).then_inc(consts, 1)
            pool.wait_ge(consts, 5)
            pool.memset(mask[CH:P, 0, CH:P], MASKED).then_inc(consts, 1)
            pool.wait_ge(consts, 6)
            pool.memset(mask[0:CH, 1, CH:P], MASKED).then_inc(consts, 1)

            def stage(b, which, unit, parity, count):
                pool.tensor_copy(staged[:, which, parity, :], ids[b][:, bass.ds(unit * UNIT, UNIT)])\
                    .then_inc(staged_sem, 1)
                pool.wait_ge(staged_sem, count)

            def gather(which, parity, i, turn):
                table, ring, landed, used = ((u_rows, u_ring, u_landed, u_used),
                                             (v_rows, v_ring, v_landed, v_used))[which]
                if not (isinstance(turn, int) and turn == 0):
                    pool.wait_ge(used, turn * RING + i % RING + 1 - RING)
                    pool.nop(nofuse=True)
                pool.indirect_dma_start(
                    out=ring[:, i % RING, :], out_offset=None, in_=table,
                    in_offset=bass.IndirectOffsetOnAxis(ap=staged[:, which, parity, i:i + 1], axis=0),
                ).then_inc(landed[i % RING], 16)

            for d in range(STEPS):
                b = d % BLOCKS
                pool.wait_ge(routed, d + 1)
                done = d * 2 * UNITS
                turn0 = d * UNITS * TURNS
                for w in range(LAG):
                    stage(b, 0, w, w % 2, done + w + 1)
                    for i in range(UNIT):
                        gather(0, w % 2, i, turn0 + w * TURNS + i // RING)
                if d == 0:
                    for w in range(LAG, LAG + 2):
                        stage(b, 0, w, w % 2, done + LAG + 2 * (w - LAG) + 1)
                        stage(b, 1, w - LAG, w % 2, done + LAG + 2 * (w - LAG) + 2)
                        for i in range(UNIT):
                            gather(0, w % 2, i, turn0 + w * TURNS + i // RING)
                            gather(1, w % 2, i, turn0 + (w - LAG) * TURNS + i // RING)
                first_pair = 2 if d == 0 else 1
                with pool.Fori(first_pair, UNITS // 2) as pair:
                    for s in range(2):
                        w = pair * 2 + s
                        stage(b, 0, w, s, pair * 4 + (done + LAG - 4 + 2 * s + 1))
                        stage(b, 1, pair * 2 + (s - LAG), s, pair * 4 + (done + LAG - 4 + 2 * s + 2))
                        for i in range(UNIT):
                            gather(0, s, i, pair * (2 * TURNS) + (turn0 + s * TURNS + i // RING))
                            gather(1, s, i, pair * (2 * TURNS) + (turn0 + (s - LAG) * TURNS + i // RING))
                for w in range(UNITS, UNITS + LAG):
                    stage(b, 1, w - LAG, w % 2, done + 2 * UNITS - LAG + (w - UNITS) + 1)
                    for i in range(UNIT):
                        gather(1, w % 2, i, turn0 + (w - LAG) * TURNS + i // RING)

        @block_ctx.tensor
        def _(pe):
            def chunk(d, c):
                n = chunk_number(d, c)
                pe.wait_ge(w_landed[n % WSLOTS], 16 * (n // WSLOTS + 1))
                return w_ring[:, n % WSLOTS, :]

            def transposes(dst_bank, tiles, done):
                for t, src in enumerate(tiles):
                    last = pe.transpose(ps[:, dst_bank * BANK + t * P:dst_bank * BANK + (t + 1) * P], src, ident[:, :])
                last.then_inc(done, 1)

            for d in range(STEPS):
                l, b = divmod(d, BLOCKS)
                if d == 0:
                    pe.wait_ge(consts, 4)
                pe.wait_ge(xm_ready, d + 1)
                transposes(0, [xm[:, k * P:(k + 1) * P] for k in range(KT)], xmT_ps)
                if b == 0:
                    pe.wait_ge(gains_in, 16 * 5 * (l + 1))
                    transposes(7, [w_sp[:, g, :] for g in range(GG)], w_spT_ps)
                pe.wait_ge(xmT_ready, d + 1)

                def project_in(c, n_bank, taken):
                    if taken:
                        pe.wait_ge(in_out, taken)
                    cols = IN_COLS[c][1]
                    w = chunk(d, c)[:, 0:KT * cols].rearrange("p (k n) -> p k n", k=KT)
                    for k in range(KT):
                        last = pe.matmul(bank(n_bank, cols), xT[:, k, :], w[:, k, :],
                                         start=(k == 0), stop=(k == KT - 1))
                    last.then_inc(w_used, 1)

                for c, n_bank in ((Q, 2), (KV, 3), (ZU, 4), (ZV, 5)):
                    project_in(c, n_bank, 0)
                pe.wait_ge(roped, d + 1)
                transposes(0, [qk[:, t, :, :].rearrange("p g d -> p (g d)") for t in range(5)], qkT_ps)
                project_in(GA0, 2, 8 * d + Q + 1)
                project_in(GA1, 3, 8 * d + KV + 1)

                pe.wait_ge(qkT_ready, d + 1)
                pe.wait_ge(in_out, 8 * d + ZV + 1)
                for g in range(NKV):
                    for t in range(GRP):
                        for kb in range(1 - b, 2):
                            c0 = (4 * BANK) + ((g * GRP + t) * 2 + kb) * P
                            keys = kT[b] if kb == 1 else kT[0]
                            last = pe.matmul(ps[:, c0:c0 + P], qT[g * HD:(g + 1) * HD, t, :],
                                             keys[g * HD:(g + 1) * HD, :], start=True, stop=True)
                last.then_inc(att_ps, 1)
                project_in(GB0, 2, 8 * d + GA0 + 1)
                project_in(GB1, 3, 8 * d + GA1 + 1)

                pe.wait_ge(ln_ready, d + 1)
                if b == 0:
                    pe.wait_ge(w_spT_ready, l + 1)
                for g in range(GG):
                    last = pe.matmul(ps[:, BANK + g * GD:BANK + (g + 1) * GD], w_spT[:, g, :],
                                     gv[:, g * GD:(g + 1) * GD], start=True, stop=True)
                last.then_inc(spat_ps, 1)

                pe.wait_ge(att_exp, d + 1)
                for hh in range(NH):
                    for kb in range(1 - b, 2):
                        c0 = (4 * BANK) + (hh * 2 + kb) * P
                        last = pe.transpose(ps[:, c0:c0 + P], probs[:, hh, kb, :], ident[:, :])
                last.then_inc(probsT_ps, 1)
                pe.wait_ge(probsT_ready, d + 1)
                for hh in range(NH):
                    g = hh // GRP
                    for kb in range(1 - b, 2):
                        vt = v_tok[b] if kb == 1 else v_tok[0]
                        last = pe.matmul(ps[:, hh * HD:(hh + 1) * HD], turned[:, hh * 2 + kb, :], vt[:, g, :],
                                         start=(kb == 1 - b), stop=(kb == 1))
                last.then_inc(pv_ps, 1)

                pe.wait_ge(in_out, 8 * d + GB1 + 1)
                pe.wait_ge(spat_ready, d + 1)
                transposes(3, [spat[:, t * P:(t + 1) * P] for t in range(4)], branchT_ps)
                pe.wait_ge(attn_ready, d + 1)
                transposes(2, [attn[:, 2 * t:2 * t + 2, :].rearrange("p h d -> p (h d)") for t in range(4)], branchT_ps)
                pe.wait_ge(branchT_ready, 2 * d + 2)
                for c, lhs, n_bank in ((W_ATTN, attnT, 4), (W_GMLP, spatT, 6)):
                    w = chunk(d, c).rearrange("p (k n) -> p k n", k=4)
                    for half in range(2):
                        for k in range(4):
                            last = pe.matmul(bank(n_bank + half), lhs[:, k, :], w[:, k, half * BANK:(half + 1) * BANK],
                                             start=(k == 0), stop=(k == 3))
                    last.then_inc(w_used, 1)

                pe.wait_ge(merged, d + 1)
                transposes(0, [xm[:, k * P:(k + 1) * P] for k in range(KT)], mergedT_ps)
                pe.wait_ge(mergedT_ready, d + 1)
                for half in range(2):
                    w = chunk(d, W_OUT0 + half).rearrange("p (k n) -> p k n", k=KT)
                    for k in range(KT):
                        last = pe.matmul(bank(2 + half), xT[:, k, :], w[:, k, :], start=(k == 0), stop=(k == KT - 1))
                    last.then_inc(w_used, 1)

                if b == 0:
                    w = chunk(d, "keys").rearrange("p (s d) -> p s d", d=KD)
                    for s in range(SIDES):
                        last = pe.transpose(ps[:, 4 * BANK + s * P:4 * BANK + (s + 1) * P], w[:, s, :], ident[:, :])
                    last.then_inc(w_used, 1)
                pe.wait_ge(xf_ready, d + 1)
                transposes(0, [xf[b][:, k * P:(k + 1) * P] for k in range(KT)], xfT_ps)
                if b == 0:
                    pe.wait_ge(keysT_ready, l + 1)
                pe.wait_ge(xfT_ready, d + 1)
                for c in range(4):
                    w = chunk(d, W_QRY0 + c).rearrange("p (k n) -> p k n", k=KT)
                    for s in range(4):
                        for k in range(KT):
                            last = pe.matmul(ps[:, (2 + c) * BANK + s * P:(2 + c) * BANK + (s + 1) * P],
                                             w[:, k, s * P:(s + 1) * P], xT[:, k, :],
                                             start=(k == 0), stop=(k == KT - 1))
                    last.then_inc(w_used, 1)
                for c, n_bank in enumerate((6, 7, 0, 1)):
                    pe.wait_ge(qry_ready, 4 * d + c + 1)
                    for s in range(4):
                        last = pe.matmul(ps[:, n_bank * BANK + s * P:n_bank * BANK + (s + 1) * P],
                                         turned[:, 4 * c + s, :], keysT[:, 4 * c + s, :], start=True, stop=True)
                    last.then_inc(side_ps, 1)

        @block_ctx.scalar
        def _(act):
            def used(d, c):
                act.wait_ge(w_used, chunk_number(d, c) + 1)

            def root(n):
                act.wait_ge(sq_in, n)
                act.activation(stat[:, 1:2], stat[:, 0:1], ACT.Sqrt).then_inc(sq_out, 1)

            def take_xm(d):
                l, b = divmod(d, BLOCKS)
                act.wait_ge(xmT_ps, d + 1)
                act.activation(xT[:, :, :], ps[:, 0:DM].rearrange("p (k n) -> p k n", k=KT), ACT.Copy)\
                    .then_inc(xmT_ready, 1)
                if b == 0:
                    act.wait_ge(w_spT_ps, l + 1)
                    src = bank(7).rearrange("p (g i) -> p g i", g=GG)
                    act.activation(w_spT[0:CH, :, :], src[0:CH, :, :], ACT.Copy)
                    act.activation(w_spT[CH:P, :, CH:P], src[CH:P, :, CH:P], ACT.Copy).then_inc(w_spT_ready, 1)

            def take_qkv(d):
                b = d % BLOCKS
                used(d, Q)
                for g in range(NKV):
                    q_g = bank(2)[:, g * GRP * HD:(g + 1) * GRP * HD].rearrange("p (t d) -> p t d", t=GRP)
                    last = act.activation(qk[:, 0:GRP, g, :], q_g, ACT.Copy)
                last.then_inc(in_out, 1)
                used(d, KV)
                act.activation(qk[:, 4, :, :], bank(3)[:, 0:P].rearrange("p (g d) -> p g d", g=NKV), ACT.Copy)
                act.activation(v_tok[b][:, :, :], bank(3)[:, P:2 * P].rearrange("p (g d) -> p g d", g=NKV), ACT.Copy)\
                    .then_inc(in_out, 1)

            def take_z(d):
                for c, n_bank, dst in ((ZU, 4, gu), (ZV, 5, gv)):
                    used(d, c)
                    act.activation(dst[:, :], bank(n_bank), ACT.Gelu).then_inc(in_out, 1)

            def take_gate(d, chunks):
                for c in chunks:
                    used(d, c)
                    k = c - GA0
                    act.activation(sig[:, k // 2, (k % 2) * BANK:(k % 2 + 1) * BANK], bank(2 + k % 2), ACT.Sigmoid)\
                        .then_inc(in_out, 1)

            def take_qkT(d):
                b = d % BLOCKS
                act.wait_ge(qkT_ps, d + 1)
                act.activation(qT[:, :, :], bank(0).rearrange("p (t n) -> p t n", t=GRP), ACT.Copy)
                act.activation(kT[b][:, :], bank(1, P), ACT.Copy).then_inc(qkT_ready, 1)

            def exps(d):
                b = d % BLOCKS
                act.wait_ge(att_max, d + 1)
                act.activation(att_m[:, 1, :], att_m[:, 1, :], ACT.Exp)
                for hh in range(NH):
                    row = probs[:, hh, 1 - b:2, :].rearrange("p s k -> p (s k)")
                    last = act.activation(row, row, ACT.Exp, bias=att_m[:, 0, hh:hh + 1],
                                          accum_out=att_m[:, 2, hh:hh + 1])
                last.then_inc(att_exp, 1)

            def take_probsT(d):
                b = d % BLOCKS
                act.wait_ge(probsT_ps, d + 1)
                src = ps[:, 4 * BANK:8 * BANK].rearrange("p (h s k) -> p h s k", h=NH, s=2)[:, :, 1 - b:2, :]
                dst = turned[:, :, :].rearrange("p (h s) k -> p h s k", s=2)[:, :, 1 - b:2, :]
                for n in range(4):
                    last = act.activation(dst[:, 2 * n:2 * n + 2, :, :], src[:, 2 * n:2 * n + 2, :, :], ACT.Copy)
                last.then_inc(probsT_ready, 1)

            def take_branchT(d):
                act.wait_ge(branchT_ps, 2 * d + 1)
                act.activation(spatT[:, :, :], bank(3).rearrange("p (t n) -> p t n", t=4), ACT.Copy)\
                    .then_inc(branchT_ready, 1)
                act.wait_ge(branchT_ps, 2 * d + 2)
                act.activation(attnT[:, :, :], bank(2).rearrange("p (t n) -> p t n", t=4), ACT.Copy)\
                    .then_inc(branchT_ready, 1)

            def take_mergedT(d):
                act.wait_ge(mergedT_ps, d + 1)
                act.activation(xT[:, :, :], ps[:, 0:DM].rearrange("p (k n) -> p k n", k=KT), ACT.Copy)\
                    .then_inc(mergedT_ready, 1)

            def take_keysT(d):
                l, b = divmod(d, BLOCKS)
                if b == 0:
                    used(d, "keys")
                    for n in range(4):
                        last = act.activation(keysT[:, 4 * n:4 * n + 4, :],
                                              bank(4 + n).rearrange("p (s k) -> p s k", s=4), ACT.Copy)
                    last.then_inc(keysT_ready, 1)

            def take_xfT(d):
                act.wait_ge(xfT_ps, d + 1)
                act.activation(xT[:, :, :], ps[:, 0:DM].rearrange("p (k n) -> p k n", k=KT), ACT.Copy)\
                    .then_inc(xfT_ready, 1)

            def take_query(d, chunks):
                for c in chunks:
                    used(d, W_QRY0 + c)
                    act.activation(turned[:, 4 * c:4 * c + 4, :], bank(2 + c).rearrange("p (s n) -> p s n", s=4),
                                   ACT.Copy).then_inc(qry_ready, 1)

            def take_sides(d):
                for c, n_bank in enumerate((6, 7, 0, 1)):
                    act.wait_ge(side_ps, 4 * d + c + 1)
                    act.activation(side_scores[:, 4 * c:4 * c + 4, :], bank(n_bank).rearrange("p (s n) -> p s n", s=4),
                                   ACT.Copy).then_inc(side_ready, 1)

            def gate_exps(d):
                act.wait_ge(gate_args, d + 1)
                act.activation(pair_s[:, :, :], pair_s[:, :, :], ACT.Exp).then_inc(gate_exp, 1)

            def gelus(e, first, last):
                with act.Fori(first, last) as w:
                    act.wait_ge(u_used, w * UNIT + (e * PICKS + UNIT))
                    act.activation(acts[:, bass.ds(w * UNIT, UNIT)], dots[:, bass.ds(w * UNIT, UNIT)], ACT.Gelu)\
                        .then_inc(gelu_done, 1)

            act.wait_ge(rope_args, 1)
            act.activation(sin[:, :, :], ang[:, :, :], ACT.Sin)
            act.activation(cos[:, :, :], turn_n[:, :, :], ACT.Sin).then_inc(rope_tab, 1)

            root(1)
            take_xm(0)
            take_qkv(0)
            take_z(0)
            root(2)
            take_qkT(0)
            take_gate(0, (GA0, GA1))
            exps(0)
            take_gate(0, (GB0, GB1))
            take_probsT(0)
            take_branchT(0)
            take_mergedT(0)
            take_keysT(0)
            root(3)
            take_xfT(0)
            take_query(0, range(4))
            take_sides(0)
            gate_exps(0)

            for e in range(STEPS - 1):
                d = e + 1
                root(3 * d + 1)
                take_xm(d)
                gelus(e, 0, 1)
                take_qkv(d)
                gelus(e, 1, 2)
                take_z(d)
                root(3 * d + 2)
                gelus(e, 2, 3)
                take_qkT(d)
                take_gate(d, (GA0, GA1))
                gelus(e, 3, 4)
                exps(d)
                take_gate(d, (GB0, GB1))
                gelus(e, 4, 5)
                take_probsT(d)
                gelus(e, 5, 6)
                take_branchT(d)
                gelus(e, 6, 7)
                take_mergedT(d)
                gelus(e, 7, 8)
                take_keysT(d)
                root(3 * d + 3)
                take_xfT(d)
                gelus(e, 8, 9)
                take_query(d, (0, 1))
                gelus(e, 9, 10)
                take_query(d, (2, 3))
                take_sides(d)
                gelus(e, 10, 14)
                gate_exps(d)
                gelus(e, 14, UNITS)

            gelus(STEPS - 1, 0, 2)
            root(3 * STEPS + 1)
            gelus(STEPS - 1, 2, UNITS)
            root(3 * STEPS + 2)

        @block_ctx.vector
        def _(vec):
            links = [0]

            def link(ins):
                links[0] += 1
                ins.then_inc(dve, 1)
                vec.wait_ge(dve, links[0])

            roots = [0]

            def rsqrt_of_stat():
                roots[0] += 1
                vec.wait_ge(sq_out, roots[0])
                link(vec.reciprocal(stat[:, 2:3], stat[:, 1:2]))
                link(vec.scalar_tensor_tensor(out=stat[:, 4:5], in0=stat[:, 2:3], scalar=stat[:, 2:3],
                                              in1=stat[:, 0:1], op0=ALU.mult, op1=ALU.mult))
                link(vec.tensor_scalar(stat[:, 4:5], stat[:, 4:5], -0.5, 1.5, ALU.mult, ALU.add))
                link(vec.tensor_tensor(stat[:, 3:4], stat[:, 2:3], stat[:, 4:5], ALU.mult))

            def mean_square(src, spare, width):
                link(vec.scalar_tensor_tensor(out=spare, in0=src, scalar=1.0, in1=src, op0=ALU.mult, op1=ALU.mult,
                                              accum_out=stat[:, 5:6]))
                vec.tensor_scalar(stat[:, 0:1], stat[:, 5:6], 1.0 / width, EPS, ALU.mult, ALU.add).then_inc(sq_in, 1)

            def norm_begin(src, dst):
                mean_square(src[:, :], dst[:, :], DM)

            def norm_end(src, dst, gain, ready):
                rsqrt_of_stat()
                vec.scalar_tensor_tensor(out=dst[:, :], in0=src[:, :], scalar=stat[:, 3:4], in1=gain[:, :],
                                         op0=ALU.mult, op1=ALU.mult).then_inc(ready, 1)

            def rope_tables():
                vec.memset(w_spT[CH:P, :, 0:CH], 0.0)
                for j in range(HALF):
                    last = vec.memset(inv_freq[:, j:j + 1], float(np.float32(THETA ** (-j / HALF))))
                link(last)
                vec.wait_ge(x_in, 16 * 6)
                for b in range(BLOCKS):
                    link(vec.tensor_copy(stat[:, 6:7], pos[:, b:b + 1]))
                    link(vec.tensor_scalar(ang[:, b, :], inv_freq[:, :], stat[:, 6:7], None, ALU.mult))
                link(vec.tensor_scalar(turn_n[:, :, :], ang[:, :, :], float(1 / (2 * np.pi)), ROUND, ALU.mult, ALU.add))
                link(vec.tensor_scalar(turn_n[:, :, :], turn_n[:, :, :], -ROUND, None, ALU.add))
                for part in two_pi_parts():
                    link(vec.scalar_tensor_tensor(out=ang[:, :, :], in0=turn_n[:, :, :], scalar=-part,
                                                  in1=ang[:, :, :], op0=ALU.mult, op1=ALU.add))
                link(vec.tensor_scalar(ang[:, :, :], ang[:, :, :], PI_DOWN, -PI_DOWN, ALU.min, ALU.max))
                link(vec.tensor_scalar(turn_n[:, :, :], ang[:, :, :], -1.0, None, ALU.mult))
                link(vec.tensor_tensor(turn_n[:, :, :], turn_n[:, :, :], ang[:, :, :], ALU.min))
                vec.tensor_scalar(turn_n[:, :, :], turn_n[:, :, :], float(np.pi / 2), None, ALU.add)\
                    .then_inc(rope_args, 1)

            def rope(d):
                b = d % BLOCKS
                vec.wait_ge(in_out, 8 * d + KV + 1)
                if d == 0:
                    vec.wait_ge(rope_tab, 1)
                heads = qk[:, :, :, :].rearrange("p t g d -> p (t g) d")
                lo, hi = heads[:, :, 0:HALF], heads[:, :, HALF:ROT]
                c = cos[:, b, :].unsqueeze(1).to_broadcast([P, 10, HALF])
                s = sin[:, b, :].unsqueeze(1).to_broadcast([P, 10, HALF])
                vec.tensor_tensor(rt[:, 0], lo, c, ALU.mult)
                vec.tensor_tensor(rt[:, 1], hi, s, ALU.mult)
                vec.tensor_tensor(rt[:, 2], hi, c, ALU.mult)
                link(vec.tensor_tensor(rt[:, 3], lo, s, ALU.mult))
                vec.tensor_tensor(lo, rt[:, 0], rt[:, 1], ALU.subtract)
                vec.tensor_tensor(hi, rt[:, 2], rt[:, 3], ALU.add).then_inc(roped, 1)

            def layer_norm_begin(d):
                vec.wait_ge(in_out, 8 * d + ZV + 1)
                if d % BLOCKS == 0:
                    vec.wait_ge(gains_in, 16 * 5 * (d // BLOCKS + 1))
                link(vec.reduce_sum(stat[:, 6:7], gv[:, :], AX))
                link(vec.tensor_scalar(stat[:, 6:7], stat[:, 6:7], -1.0 / GW, None, ALU.mult))
                link(vec.tensor_scalar(gv[:, :], gv[:, :], stat[:, 6:7], None, ALU.add))
                mean_square(gv[:, :], spat[:, :], GW)

            def layer_norm_end(d):
                rsqrt_of_stat()
                link(vec.scalar_tensor_tensor(out=gv[:, :], in0=gv[:, :], scalar=stat[:, 3:4], in1=ln_g[:, :],
                                              op0=ALU.mult, op1=ALU.mult))
                vec.tensor_tensor(gv[:, :], gv[:, :], ln_b[:, :], ALU.add).then_inc(ln_ready, 1)

            def softmax_args(d):
                l, b = divmod(d, BLOCKS)
                if d == 0:
                    vec.wait_ge(consts, 7)
                vec.wait_ge(att_ps, d + 1)
                cols = (1 + b) * P
                src = ps[:, 4 * BANK:8 * BANK].rearrange("p (h k) -> p h k", h=NH)[:, :, 2 * P - cols:2 * P]
                dst = probs[:, :, :, :].rearrange("p h s k -> p h (s k)")[:, :, 2 * P - cols:2 * P]
                m = mask[:, :, :].rearrange("p s k -> p (s k)")[:, 2 * P - cols:2 * P]
                m = m.unsqueeze(1).to_broadcast([P, NH, cols])
                link(vec.scalar_tensor_tensor(out=dst, in0=src, scalar=float(HD ** -0.5), in1=m,
                                              op0=ALU.mult, op1=ALU.add))
                link(vec.tensor_reduce(att_m[:, 0, :], dst, AX, ALU.max))
                link(vec.tensor_tensor(att_m[:, 0, :], att_m[:, 0, :], sinks[:, l, :], ALU.max))
                link(vec.tensor_tensor(att_m[:, 1, :], sinks[:, l, :], att_m[:, 0, :], ALU.subtract))
                vec.tensor_scalar(att_m[:, 0, :], att_m[:, 0, :], -1.0, None, ALU.mult).then_inc(att_max, 1)

            def spatial_gate(d):
                l = d // BLOCKS
                vec.wait_ge(spat_ps, d + 1)
                for g in range(GG):
                    last = vec.scalar_tensor_tensor(
                        out=spat[:, g * GD:(g + 1) * GD], in0=ps[:, BANK + g * GD:BANK + (g + 1) * GD],
                        scalar=b_sp[:, l, g:g + 1], in1=gu[:, g * GD:(g + 1) * GD], op0=ALU.add, op1=ALU.mult)
                last.then_inc(spat_ready, 1)

            def attention_out(d):
                vec.wait_ge(pv_ps, d + 1)
                link(vec.tensor_tensor(att_m[:, 3, :], att_m[:, 2, :], att_m[:, 1, :], ALU.add))
                link(vec.reciprocal(att_m[:, 3, :], att_m[:, 3, :]))
                vec.tensor_tensor(attn[:, :, :], bank(0).rearrange("p (h d) -> p h d", h=NH),
                                  att_m[:, 3, :].unsqueeze(2).to_broadcast([P, NH, HD]), ALU.mult)\
                    .then_inc(attn_ready, 1)

            def merge(d):
                vec.wait_ge(w_used, chunk_number(d, W_GMLP) + 1)
                vec.tensor_tensor(sig[:, 0, :], sig[:, 0, :], ps[:, 4 * BANK:6 * BANK], ALU.mult)
                link(vec.tensor_tensor(sig[:, 1, :], sig[:, 1, :], ps[:, 6 * BANK:8 * BANK], ALU.mult))
                vec.tensor_tensor(xm[:, :], sig[:, 0, :], sig[:, 1, :], ALU.add).then_inc(merged, 1)

            def add_mixer(d):
                b = d % BLOCKS
                vec.wait_ge(w_used, chunk_number(d, W_OUT1) + 1)
                link(vec.tensor_tensor(h[b][:, :], h[b][:, :], ps[:, 2 * BANK:4 * BANK], ALU.add))
                norm_begin(h[b], xf[b])

            def top16(scores, values, indices):
                link(vec.max(values[:, 0:8], scores))
                vec.max_index(indices[:, 0:8], values[:, 0:8], scores)
                link(vec.match_replace(scores, values[:, 0:8], scores, LOWEST))
                link(vec.max(values[:, 8:16], scores))
                return vec.max_index(indices[:, 8:16], values[:, 8:16], scores)

            def side_top(d, sides):
                for s in sides:
                    vec.wait_ge(side_ready, 4 * d + s // 4 + 1)
                    last = top16(side_scores[:, s, :], top_v[:, s, :], top_i[:, s, :])
                link(last)

            def pair_top(heads):
                for hh in heads:
                    c = cand[:, hh % 2, :, :]
                    link(vec.tensor_tensor(c, top_v[:, 2 * hh, :].unsqueeze(2).to_broadcast([P, TOPK, TOPK]),
                                           top_v[:, 2 * hh + 1, :].unsqueeze(1).to_broadcast([P, TOPK, TOPK]), ALU.add))
                    last = top16(c.rearrange("p a b -> p (a b)"), pair_s[:, hh, :],
                                 pair_i[:, hh * TOPK:(hh + 1) * TOPK])
                link(last)

            def gate_arguments(d):
                link(vec.tensor_copy(gsum[:, :], pair_s[:, :, 0]))
                vec.tensor_tensor(pair_s[:, :, :], pair_s[:, :, :],
                                  gsum[:, :].unsqueeze(2).to_broadcast([P, PH, TOPK]), ALU.subtract)\
                    .then_inc(gate_args, 1)
                vec.tensor_single_scalar(pair_ab[:, 0, :], pair_i[:, :], 4, ALU.logical_shift_right)
                link(vec.tensor_single_scalar(pair_ab[:, 1, :], pair_i[:, :], TOPK - 1, ALU.bitwise_and))

            def look_up(side):
                one_hot = turned[:, :, :].rearrange("p s n -> p (s n)").rearrange("p (k m) -> p k m", m=TOPK)
                link(vec.tensor_tensor(one_hot, pair_ab[:, side, :].unsqueeze(2).to_broadcast([P, PICKS, TOPK]),
                                       iota[:, :].unsqueeze(1).to_broadcast([P, PICKS, TOPK]), ALU.is_equal))
                per_head = turned[:, :, :].rearrange("p s n -> p (s n)")\
                    .rearrange("p (h j m) -> p h j m", h=PH, m=TOPK)
                places = top_i[:, :, :].rearrange("p (h t) m -> p h t m", t=2)[:, :, side, :]
                link(vec.tensor_tensor(per_head, per_head, places.unsqueeze(2).to_broadcast([P, PH, TOPK, TOPK]),
                                       ALU.mult))
                link(vec.reduce_sum(key_ab[:, side, :], one_hot, AX))

            def route(d):
                l, b = divmod(d, BLOCKS)
                link(vec.scalar_tensor_tensor(out=key_ab[:, 2, :], in0=key_ab[:, 0, :], scalar=float(NK),
                                              in1=key_ab[:, 1, :], op0=ALU.mult, op1=ALU.add))
                link(vec.tensor_scalar(ids[b][:, :], key_ab[:, 2, :], float(l * NE), None, ALU.add))
                vec.wait_ge(gate_exp, d + 1)
                link(vec.reduce_sum(gsum[:, :], pair_s[:, :, :], AX))
                link(vec.reciprocal(gsum[:, :], gsum[:, :]))
                vec.tensor_tensor(gates[b][:, :].rearrange("p (h j) -> p h j", h=PH), pair_s[:, :, :],
                                  gsum[:, :].unsqueeze(2).to_broadcast([P, PH, TOPK]), ALU.mult).then_inc(routed, 1)

            def u_pick(e, w, i):
                vec.wait_ge(u_landed[i % RING], w * (16 * TURNS) + 16 * (e * UNITS * TURNS + i // RING + 1))
                vec.scalar_tensor_tensor(out=junk[:, :], in0=xf[e % BLOCKS][:, :], scalar=1.0,
                                         in1=u_ring[:, i % RING, :], op0=ALU.mult, op1=ALU.mult,
                                         accum_out=dots[:, bass.ds(w * UNIT + i, 1)]).then_inc(u_used, 1)

            def coefficients(e, w):
                cols = bass.ds(w * UNIT - LAG * UNIT, UNIT)
                vec.wait_ge(gelu_done, w + (e * UNITS - LAG + 1))
                vec.tensor_tensor(coef[:, cols], acts[:, cols], gates[e % BLOCKS][:, cols], ALU.mult)\
                    .then_inc(coef_ready, 1)
                vec.wait_ge(coef_ready, w + (e * UNITS - LAG + 1))

            def v_pick(e, w, i):
                hb = h[e % BLOCKS]
                vec.wait_ge(v_landed[i % RING], w * (16 * TURNS) + 16 * ((e * UNITS - LAG) * TURNS + i // RING + 1))
                vec.scalar_tensor_tensor(out=hb[:, :], in0=v_ring[:, i % RING, :],
                                         scalar=coef[:, bass.ds(w * UNIT + (i - LAG * UNIT), 1)],
                                         in1=hb[:, :], op0=ALU.mult, op1=ALU.add).then_inc(v_used, 1)

            def units(e, first, last):
                with vec.Fori(first, last) as w:
                    if first >= LAG:
                        coefficients(e, w)
                    for i in range(UNIT):
                        if last <= UNITS:
                            u_pick(e, w, i)
                        if first >= LAG:
                            if i > 0:
                                vec.wait_ge(v_used, w * UNIT + (e * PICKS - LAG * UNIT + i))
                            v_pick(e, w, i)
                        if last <= UNITS:
                            vec.wait_ge(u_used, w * UNIT + (e * PICKS + i + 1))
                    if first >= LAG:
                        vec.wait_ge(v_used, w * UNIT + (e * PICKS - LAG * UNIT + UNIT))

            rope_tables()
            norm_begin(h[0], xm)
            vec.wait_ge(gains_in, 16 * 5)
            norm_end(h[0], xm, gain_mix, xm_ready)
            rope(0)
            layer_norm_begin(0)
            layer_norm_end(0)
            softmax_args(0)
            spatial_gate(0)
            attention_out(0)
            merge(0)
            add_mixer(0)
            norm_end(h[0], xf[0], gain_ffn, xf_ready)
            side_top(0, range(SIDES))
            pair_top(range(PH))
            gate_arguments(0)
            look_up(0)
            look_up(1)
            route(0)

            for e in range(STEPS - 1):
                d, b = e + 1, (e + 1) % BLOCKS
                norm_begin(h[b], xm)
                if b == 0:
                    vec.wait_ge(gains_in, 16 * 5 * (d // BLOCKS + 1))
                norm_end(h[b], xm, gain_mix, xm_ready)
                units(e, 0, 2)
                rope(d)
                units(e, 2, 3)
                layer_norm_begin(d)
                layer_norm_end(d)
                units(e, 3, 4)
                softmax_args(d)
                units(e, 4, 5)
                spatial_gate(d)
                units(e, 5, 6)
                attention_out(d)
                units(e, 6, 7)
                merge(d)
                units(e, 7, 8)
                add_mixer(d)
                norm_end(h[b], xf[b], gain_ffn, xf_ready)
                units(e, 8, 11)
                side_top(d, range(0, 8))
                units(e, 11, 12)
                side_top(d, range(8, 16))
                units(e, 12, 13)
                pair_top(range(0, 4))
                units(e, 13, 14)
                pair_top(range(4, 8))
                gate_arguments(d)
                units(e, 14, 15)
                look_up(0)
                units(e, 15, UNITS)
                look_up(1)
                route(d)
                units(e, UNITS, UNITS + LAG)

            e = STEPS - 1
            units(e, 0, 2)
            norm_begin(h[0], xf[0])
            vec.wait_ge(final_in, 16)
            norm_end(h[0], xf[0], gain_mix, y_ready)
            units(e, 2, UNITS)
            units(e, UNITS, UNITS + LAG)
            norm_begin(h[1], xf[1])
            norm_end(h[1], xf[1], gain_mix, y_ready)


_INS = ["x", "positions", "norm_mix_g", "w_in", "attn_sinks", "gmlp_ln_g", "gmlp_ln_b", "w_spatial", "b_spatial",
        "w_attn_branch", "w_gmlp_branch", "w_out", "norm_ffn_g", "peer_w_query", "peer_sub_keys", "peer_u", "peer_v",
        "final_norm_g"]


def kernel(**inputs):
    import concourse.bacc as _bacc
    from concourse.bass_utils import run_bass_kernel_spmd as _run

    nc = _bacc.Bacc("TRN2", target_bir_lowering=False, num_devices=1)
    arrays, args = {}, []
    for name in _INS:
        a = np.ascontiguousarray(inputs[name])
        arrays[f"in_{name}"] = a
        args.append(nc.dram_tensor(f"in_{name}", a.shape, mybir.dt.from_np(a.dtype), kind="ExternalInput").ap())
    args.append(nc.dram_tensor("out_trunk", (1, BLOCKS * P, DM), F32, kind="ExternalOutput").ap())
    build(nc, *args)
    r = _run(nc, [arrays], core_ids=[0])
    return r.results[0]["out_trunk"]
```

```python
from contextlib import ExitStack

import numpy as np

import concourse.bass as bass
from concourse import mybir

F32 = mybir.dt.float32
I32 = mybir.dt.int32
U32 = mybir.dt.uint32
ALU = mybir.AluOpType
ACT = mybir.ActivationFunctionType
AX = mybir.AxisListType.X

P = 128
BLOCKS = 2
DM = 1024
KT = DM // P
DEPTH = 2
STEPS = DEPTH * BLOCKS
CH = 64
NH, NKV, HD = 8, 2, 64
GRP = NH // NKV
ROT = HD // 4
HALF = ROT // 2
THETA = 500000.0
GW, GG = 512, 4
GD = GW // GG
PH, NK, KD = 8, 128, 128
SIDES = 2 * PH
NE = NK * NK
TOPK = 16
PICKS = PH * TOPK
EPS = 1e-6
MASKED = -1e30
LOWEST = -3.0e38
BANK = 512

UNIT = 8
UNITS = PICKS // UNIT
LAG = 2
RING = 8
TURNS = UNIT // RING
WSLOTS = 4

PI_DOWN = float(np.nextafter(np.float32(np.pi), np.float32(0)))
ROUND = float(1.5 * 2 ** 23)


def two_pi_parts():
    rest, parts = 2 * np.pi, []
    for _ in range(3):
        scale = 2.0 ** (np.floor(np.log2(rest)) - 7)
        parts.append(float(np.floor(rest / scale) * scale))
        rest -= parts[-1]
    return parts + [float(rest)]


IN_COLS = [(0, 512), (512, 256), (768, 512), (1280, 512), (1792, 512), (2304, 512), (2816, 512), (3328, 512)]
Q, KV, ZU, ZV, GA0, GA1, GB0, GB1, W_ATTN, W_GMLP, W_OUT0, W_OUT1, W_QRY0 = range(13)
KEYS = W_QRY0 + 4
ROUTES = 4
R_HEADS = PH // ROUTES
R_SIDES = SIDES // ROUTES
R_PICKS = PICKS // ROUTES


def chunk_order():
    dense = [Q, KV, ZU, ZV, GA0, GA1, GB0, GB1]
    tail = [W_GMLP, W_ATTN, W_OUT0, W_OUT1]
    query = [W_QRY0 + c for c in range(4)]
    order = [(0, c) for c in dense] + [(1, Q), (1, KV), (0, W_GMLP), (0, W_ATTN), (1, ZU), (0, W_OUT0), (0, W_OUT1),
                                       (1, ZV), (0, KEYS)] + [(0, c) for c in query]
    order += [(1, c) for c in [GA0, GA1, GB0, GB1] + tail + query]
    order += [(2, c) for c in dense + tail + [KEYS] + query]
    order += [(3, c) for c in dense + tail + query]
    return order


ORDER = chunk_order()
NUMBER = {dc: n for n, dc in enumerate(ORDER)}
IN_ORDER = [dc for dc in ORDER if dc[1] <= GB1]
IN_BANK = {dc: 2 + n % 2 for n, dc in enumerate(IN_ORDER)}
IN_BEFORE = {dc: IN_ORDER[n - 2] for n, dc in enumerate(IN_ORDER) if n >= 2}


def halves_used(d, c):
    return 2 * NUMBER[d, c] + 2


def build(nc, x, positions, norm_mix_g, w_in, attn_sinks, gmlp_ln_g, gmlp_ln_b, w_spatial, b_spatial,
          w_attn_branch, w_gmlp_branch, w_out, norm_ffn_g, peer_w_query, peer_sub_keys, peer_u, peer_v,
          final_norm_g, out):
    u_rows = peer_u.rearrange("l e d -> (l e) d")
    v_rows = peer_v.rearrange("l e d -> (l e) d")

    with ExitStack() as ctx:
        def sb(name, shape, dt=F32):
            return ctx.enter_context(nc.sbuf_tensor(name, shape, dt))

        def sem(name):
            return ctx.enter_context(nc.semaphore(name))

        h = [sb(f"h{b}", [P, DM]) for b in range(BLOCKS)]
        xf = [sb(f"xf{b}", [P, DM]) for b in range(BLOCKS)]
        xT = [sb(f"xT{b}", [P, KT, P]) for b in range(BLOCKS)]
        qk = sb("qk", [P, 5, 2, HD])
        v_tok = [sb(f"v_tok{b}", [P, NKV, HD]) for b in range(BLOCKS)]
        qT = sb("qT", [P, GRP, P])
        kT = [sb(f"kT{b}", [P, P]) for b in range(BLOCKS)]
        gu = sb("gu", [P, GW])
        gv = sb("gv", [P, GW])
        spatT = gu[:, :].rearrange("p (t n) -> p t n", t=4)
        attnT = gv[:, :].rearrange("p (t n) -> p t n", t=4)
        sig = sb("sig", [P, 2, DM])
        probs = sb("probs", [P, NH, 2, P])
        side_scores = probs[:, :, :, :].rearrange("p h s k -> p (h s) k")
        turned = sb("turned", [P, SIDES, P])
        attn = sb("attn", [P, NH, HD])
        spat = sb("spat", [P, GW])
        rt = sb("rt", [P, 4, 10, HALF])
        keysT = sb("keysT", [P, SIDES, NK])
        w_sp = sb("w_sp", [P, GG, P])
        w_spT = sb("w_spT", [P, GG, P])
        gain_mix = sb("gain_mix", [P, DM])
        gain_ffn = sb("gain_ffn", [P, DM])
        ln_g = sb("ln_g", [P, GW])
        ln_b = sb("ln_b", [P, GW])
        b_sp = sb("b_sp", [P, DEPTH, GG])
        sinks = sb("sinks", [P, DEPTH, NH])
        mask = sb("mask", [P, 2, P])
        ident = sb("ident", [P, P])
        pos = sb("pos", [P, BLOCKS], I32)
        inv_freq = sb("inv_freq", [P, HALF])
        ang = sb("ang", [P, BLOCKS, HALF])
        turn_n = sb("turn_n", [P, BLOCKS, HALF])
        cos = sb("cos", [P, BLOCKS, HALF])
        sin = sb("sin", [P, BLOCKS, HALF])
        iota = sb("iota", [P, TOPK])
        stat = sb("stat", [P, 8])
        att_m = sb("att_m", [P, 4, NH])
        top_v = sb("top_v", [P, SIDES, TOPK])
        top_i = sb("top_i", [P, SIDES, TOPK], U32)
        cand = sb("cand", [P, 2, TOPK, TOPK])
        pair_s = sb("pair_s", [P, PH, TOPK])
        pair_i = sb("pair_i", [P, PICKS], U32)
        pair_ab = sb("pair_ab", [P, 2, PICKS], U32)
        one_hot = sb("one_hot", [P, 2, R_PICKS, TOPK])
        key_ab = sb("key_ab", [P, 3, PICKS])
        gsum = sb("gsum", [P, PH])
        gates = [sb(f"gates{b}", [P, PICKS]) for b in range(BLOCKS)]
        ids = [sb(f"ids{b}", [P, PICKS], I32) for b in range(BLOCKS)]
        dots = sb("dots", [P, PICKS])
        acts = sb("acts", [P, PICKS])
        coef = sb("coef", [P, PICKS])
        junk = sb("junk", [P, DM])
        staged = sb("staged", [P, 2, 2, UNIT], I32)
        u_ring = sb("u_ring", [P, RING, DM])
        v_ring = sb("v_ring", [P, RING, DM])
        w_ring = sb("w_ring", [P, WSLOTS, KT * BANK // 2])
        ps = ctx.enter_context(nc.psum_tensor("ps", [P, 8 * BANK], F32))

        def bank(n, width=BANK):
            return ps[:, n * BANK:n * BANK + width]

        def att_psum(b):
            return ps[:, 4 * BANK:4 * BANK + NH * (1 + b) * P].rearrange("p (h s k) -> p h s k", h=NH, s=1 + b)

        x0_in = sem("x0_in")
        x1_in = sem("x1_in")
        small_in = sem("small_in")
        mix_in = sem("mix_in")
        gains_in = sem("gains_in")
        w_landed = [sem(f"w_landed{s}") for s in range(WSLOTS)]
        w_used = sem("w_used")
        out_done = sem("out_done")
        consts = sem("consts")
        rope_args = sem("rope_args")
        rope_tab = sem("rope_tab")
        dve = sem("dve")
        sq_in = sem("sq_in")
        sq_out = sem("sq_out")
        xm_ready = sem("xm_ready")
        xmT_ps = sem("xmT_ps")
        xmT_ready = sem("xmT_ready")
        w_spT_ps = sem("w_spT_ps")
        w_spT_ready = sem("w_spT_ready")
        in_out = [sem(f"in_out{b}") for b in range(BLOCKS)]
        roped = sem("roped")
        qkT_ps = sem("qkT_ps")
        qkT_ready = sem("qkT_ready")
        att_ps = sem("att_ps")
        att_max = sem("att_max")
        att_exp = sem("att_exp")
        probsT_ps = sem("probsT_ps")
        probsT_ready = sem("probsT_ready")
        pv_ps = sem("pv_ps")
        attn_ready = sem("attn_ready")
        ln_ready = sem("ln_ready")
        spat_ps = sem("spat_ps")
        spat_ready = sem("spat_ready")
        branchT_ps = sem("branchT_ps")
        branchT_ready = sem("branchT_ready")
        merged = sem("merged")
        mergedT_ps = sem("mergedT_ps")
        mergedT_ready = sem("mergedT_ready")
        xf_ready = sem("xf_ready")
        xfT_ps = sem("xfT_ps")
        xfT_ready = sem("xfT_ready")
        keysT_ready = sem("keysT_ready")
        qry_ready = sem("qry_ready")
        side_ps = sem("side_ps")
        side_ready = sem("side_ready")
        gate_args = sem("gate_args")
        gate_exp = sem("gate_exp")
        routed = sem("routed")
        staged_sem = sem("staged")
        u_landed = [sem(f"u_landed{s}") for s in range(RING)]
        v_landed = [sem(f"v_landed{s}") for s in range(RING)]
        u_used = sem("u_used")
        v_used = sem("v_used")
        gelu_done = sem("gelu_done")
        coef_ready = sem("coef_ready")
        y_ready = sem("y_ready")

        block_ctx = ctx.enter_context(nc.Block())

        @block_ctx.sync
        def _(sp):
            def load_layer(l):
                sp.dma_start(w_sp[:, :, :], w_spatial[l].rearrange("g i j -> i g j")).then_inc(gains_in, 16)
                sp.dma_start(ln_g[:, :], gmlp_ln_g[l, :].partition_broadcast(P)).then_inc(gains_in, 16)
                sp.dma_start(ln_b[:, :], gmlp_ln_b[l, :].partition_broadcast(P)).then_inc(gains_in, 16)
                sp.dma_start(gain_ffn[:, :], norm_ffn_g[l, :].partition_broadcast(P)).then_inc(gains_in, 16)

            def load_half(n, cols, src):
                if n >= WSLOTS:
                    sp.wait_ge(w_used, n - WSLOTS + 1)
                dst = w_ring[:, n % WSLOTS, 0:src.shape[1] * cols].rearrange("p (k n) -> p k n", n=cols)
                sp.dma_start(dst, src).then_inc(w_landed[n % WSLOTS], 16)

            def load_weights(first, last):
                for n in range(first, last):
                    d, c = ORDER[n]
                    l = d // BLOCKS
                    for j in range(2):
                        if c <= GB1:
                            c0, cols = IN_COLS[c]
                            w = w_in[l, j * DM // 2:(j + 1) * DM // 2, c0:c0 + cols]
                        elif c in (W_ATTN, W_GMLP):
                            cols = BANK
                            w = (w_attn_branch if c == W_ATTN else w_gmlp_branch)[l, :, j * cols:(j + 1) * cols]
                        elif c in (W_OUT0, W_OUT1):
                            c0, cols = (c - W_OUT0) * BANK, BANK
                            w = w_out[l, j * DM // 2:(j + 1) * DM // 2, c0:c0 + cols]
                        elif c == KEYS:
                            load_half(2 * n + j, KD, peer_sub_keys[l, j * PH // 2:(j + 1) * PH // 2]
                                      .rearrange("h t k d -> k (h t) d"))
                            continue
                        else:
                            cols = BANK // 2
                            c0 = (c - W_QRY0) * BANK + j * cols
                            w = peer_w_query[l, :, c0:c0 + cols]
                        load_half(2 * n + j, cols, w.rearrange("(k p) n -> p k n", p=P))

            sp.dma_start(h[0][:, :], x[0, 0:P, :]).then_inc(x0_in, 16)
            sp.dma_start(pos[:, :], positions[0].rearrange("(b p) -> p b", p=P),
                         allow_slow_non_contiguous=True).then_inc(x0_in, 16)
            sp.dma_start(gain_mix[:, :], norm_mix_g[0, :].partition_broadcast(P)).then_inc(mix_in, 16)
            load_weights(0, 1)
            sp.dma_start(h[1][:, :], x[0, P:2 * P, :]).then_inc(x1_in, 16)
            load_weights(1, 2)
            load_layer(0)
            sp.dma_start(sinks[:, :, :], attn_sinks.partition_broadcast(P)).then_inc(small_in, 16)
            for l in range(DEPTH):
                sp.dma_start(b_sp[:, l, :], b_spatial[l].rearrange("g i -> i g"),
                             allow_slow_non_contiguous=True).then_inc(small_in, 16)
            load_weights(2, NUMBER[2, Q])
            sp.wait_ge(xf_ready, 2)
            sp.dma_start(gain_mix[:, :], norm_mix_g[1, :].partition_broadcast(P)).then_inc(mix_in, 16)
            load_layer(1)
            load_weights(NUMBER[2, Q], len(ORDER))
            sp.wait_ge(xm_ready, 4)
            sp.dma_start(gain_mix[:, :], final_norm_g.partition_broadcast(P)).then_inc(mix_in, 16)
            for b in range(BLOCKS):
                sp.wait_ge(y_ready, b + 1)
                sp.dma_start(out[0, b * P:(b + 1) * P, :], xf[b][:, :]).then_inc(out_done, 16)
            sp.wait_ge(out_done, 16 * BLOCKS)

        @block_ctx.gpsimd
        def _(pool):
            pool.memset(ident[:, :], 0.0).then_inc(consts, 1)
            pool.memset(mask[:, :, :], 0.0).then_inc(consts, 1)
            pool.iota(iota[:, :], [[1, TOPK]], base=0, channel_multiplier=0,
                      allow_small_or_imprecise_dtypes=True).then_inc(consts, 1)
            pool.wait_ge(consts, 3)
            pool.affine_select(out=ident[:, :], in_=ident[:, :], compare_op=ALU.not_equal, fill=1.0, base=0,
                               pattern=[[-1, P]], channel_multiplier=1).then_inc(consts, 1)
            pool.memset(mask[:, 0, 0:CH], MASKED).then_inc(consts, 1)
            pool.wait_ge(consts, 5)
            pool.memset(mask[CH:P, 0, CH:P], MASKED).then_inc(consts, 1)
            pool.wait_ge(consts, 6)
            pool.memset(mask[0:CH, 1, CH:P], MASKED).then_inc(consts, 1)

            def stage(b, which, unit, parity, count):
                pool.tensor_copy(staged[:, which, parity, :], ids[b][:, bass.ds(unit * UNIT, UNIT)])\
                    .then_inc(staged_sem, 1)
                pool.wait_ge(staged_sem, count)

            def gather(which, parity, i, turn):
                table, ring, landed, used = ((u_rows, u_ring, u_landed, u_used),
                                             (v_rows, v_ring, v_landed, v_used))[which]
                if not (isinstance(turn, int) and turn == 0):
                    pool.wait_ge(used, turn * RING + i % RING + 1 - RING)
                    pool.nop(nofuse=True)
                pool.indirect_dma_start(
                    out=ring[:, i % RING, :], out_offset=None, in_=table,
                    in_offset=bass.IndirectOffsetOnAxis(ap=staged[:, which, parity, i:i + 1], axis=0),
                ).then_inc(landed[i % RING], 16)

            for d in range(STEPS):
                b = d % BLOCKS
                pool.wait_ge(routed, 2 * ROUTES * d + 1)
                done = d * 2 * UNITS
                turn0 = d * UNITS * TURNS
                for w in range(LAG):
                    stage(b, 0, w, w % 2, done + w + 1)
                    for i in range(UNIT):
                        gather(0, w % 2, i, turn0 + w * TURNS + i // RING)
                if d == 0:
                    pool.wait_ge(routed, 2)
                    for w in range(LAG, LAG + 2):
                        stage(b, 0, w, w % 2, done + LAG + 2 * (w - LAG) + 1)
                        stage(b, 1, w - LAG, w % 2, done + LAG + 2 * (w - LAG) + 2)
                        for i in range(UNIT):
                            gather(0, w % 2, i, turn0 + w * TURNS + i // RING)
                            gather(1, w % 2, i, turn0 + (w - LAG) * TURNS + i // RING)
                first_pair = 2 if d == 0 else 1
                with pool.Fori(first_pair, UNITS // 2) as pair:
                    pool.wait_ge(routed, pair + (2 * ROUTES * d + 1))
                    pool.nop(nofuse=True)
                    for s in range(2):
                        w = pair * 2 + s
                        stage(b, 0, w, s, pair * 4 + (done + LAG - 4 + 2 * s + 1))
                        stage(b, 1, pair * 2 + (s - LAG), s, pair * 4 + (done + LAG - 4 + 2 * s + 2))
                        for i in range(UNIT):
                            gather(0, s, i, pair * (2 * TURNS) + (turn0 + s * TURNS + i // RING))
                            gather(1, s, i, pair * (2 * TURNS) + (turn0 + (s - LAG) * TURNS + i // RING))
                for w in range(UNITS, UNITS + LAG):
                    stage(b, 1, w - LAG, w % 2, done + 2 * UNITS - LAG + (w - UNITS) + 1)
                    for i in range(UNIT):
                        gather(1, w % 2, i, turn0 + (w - LAG) * TURNS + i // RING)

        @block_ctx.tensor
        def _(pe):
            def half(d, c, j, cols):
                n = 2 * NUMBER[d, c] + j
                pe.wait_ge(w_landed[n % WSLOTS], 16 * (n // WSLOTS + 1))
                return w_ring[:, n % WSLOTS, :].rearrange("p (k n) -> p k n", n=cols)

            def project(d, c, dst, lhs, cols):
                for j in range(2):
                    w = half(d, c, j, cols)
                    for k in range(4):
                        last = pe.matmul(dst, lhs[:, 4 * j + k, :], w[:, k, :], start=(j + k == 0),
                                         stop=(j == 1 and k == 3))
                    last.then_inc(w_used, 1)

            def transposes(dst_bank, tiles, done):
                for t, src in enumerate(tiles):
                    last = pe.transpose(ps[:, dst_bank * BANK + t * P:dst_bank * BANK + (t + 1) * P], src, ident[:, :])
                last.then_inc(done, 1)

            def xm_transposes(d):
                l, b = divmod(d, BLOCKS)
                pe.wait_ge(xm_ready, d + 1)
                if d == 1:
                    pe.wait_ge(xmT_ready, 1)
                if d >= 2:
                    pe.wait_ge(side_ready, ROUTES * d)
                transposes(0, [xf[b][:, k * P:(k + 1) * P] for k in range(KT)], xmT_ps)
                if b == 0:
                    pe.wait_ge(gains_in, 16 * 4 * (l + 1))
                    transposes(7, [w_sp[:, g, :] for g in range(GG)], w_spT_ps)

            def project_in(d, chunks):
                b = d % BLOCKS
                pe.wait_ge(xmT_ready, d + 1)
                for c in chunks:
                    if (d, c) in IN_BEFORE:
                        d0, c0 = IN_BEFORE[d, c]
                        pe.wait_ge(in_out[d0 % BLOCKS], 8 * (d0 // BLOCKS) + c0 + 1)
                    cols = IN_COLS[c][1]
                    project(d, c, bank(IN_BANK[d, c], cols), xT[b], cols)

            def qk_transposes(d):
                pe.wait_ge(roped, d + 1)
                if d == 0:
                    pe.wait_ge(xmT_ready, 2)
                if d == 1:
                    pe.wait_ge(side_ready, ROUTES)
                transposes(0, [qk[:, t, :, :].rearrange("p g d -> p (g d)") for t in range(5)], qkT_ps)

            def scores(d):
                b = d % BLOCKS
                pe.wait_ge(qkT_ready, d + 1)
                if d > 0:
                    pe.wait_ge(qry_ready, ROUTES * d)
                dst = att_psum(b)
                for g in range(NKV):
                    for t in range(GRP):
                        for s in range(1 + b):
                            keys = kT[s]
                            last = pe.matmul(dst[:, g * GRP + t, s, :], qT[g * HD:(g + 1) * HD, t, :],
                                             keys[g * HD:(g + 1) * HD, :], start=True, stop=True)
                last.then_inc(att_ps, 1)

            def spatial(d):
                l, b = divmod(d, BLOCKS)
                pe.wait_ge(ln_ready, d + 1)
                pe.wait_ge(w_spT_ready, l + 1)
                for g in range(GG):
                    last = pe.matmul(bank(1)[:, g * GD:(g + 1) * GD], w_spT[:, g, :],
                                     gv[:, g * GD:(g + 1) * GD], start=True, stop=True)
                last.then_inc(spat_ps, 1)

            def probs_transposes(d):
                b = d % BLOCKS
                pe.wait_ge(att_exp, d + 1)
                dst = att_psum(b)
                for hh in range(NH):
                    for s in range(1 + b):
                        last = pe.transpose(dst[:, hh, s, :], probs[:, hh, 1 - b + s, :], ident[:, :])
                last.then_inc(probsT_ps, 1)

            def probs_values(d):
                b = d % BLOCKS
                pe.wait_ge(probsT_ready, d + 1)
                for hh in range(NH):
                    g = hh // GRP
                    for kb in range(1 - b, 2):
                        vt = v_tok[b] if kb == 1 else v_tok[0]
                        last = pe.matmul(ps[:, hh * HD:(hh + 1) * HD], turned[:, hh * 2 + kb, :], vt[:, g, :],
                                         start=(kb == 1 - b), stop=(kb == 1))
                last.then_inc(pv_ps, 1)

            def branch(d, c, lhs, n_bank):
                for j in range(2):
                    w = half(d, c, j, BANK)
                    for k in range(4):
                        last = pe.matmul(bank(n_bank + j), lhs[:, k, :], w[:, k, :], start=(k == 0), stop=(k == 3))
                    last.then_inc(w_used, 1)

            def gmlp_branch(d):
                pe.wait_ge(spat_ready, d + 1)
                transposes(1, [spat[:, t * P:(t + 1) * P] for t in range(4)], branchT_ps)
                pe.wait_ge(branchT_ready, 2 * d + 1)
                branch(d, W_GMLP, spatT, 6)

            def attn_branch(d):
                pe.wait_ge(attn_ready, d + 1)
                transposes(0, [attn[:, 2 * t:2 * t + 2, :].rearrange("p h d -> p (h d)") for t in range(4)], branchT_ps)
                pe.wait_ge(branchT_ready, 2 * d + 2)
                branch(d, W_ATTN, attnT, 4)

            def project_out(d):
                b = d % BLOCKS
                pe.wait_ge(merged, d + 1)
                transposes(0, [sig[:, 0, k * P:(k + 1) * P] for k in range(KT)], mergedT_ps)
                pe.wait_ge(mergedT_ready, d + 1)
                for n in range(2):
                    project(d, W_OUT0 + n, bank(4 + n), xT[b], BANK)

            def key_transposes(d):
                for j in range(2):
                    if j == 1:
                        pe.wait_ge(keysT_ready, 2 * (d // BLOCKS) + 1)
                    w = half(d, KEYS, j, KD)
                    for s in range(SIDES // 2):
                        last = pe.transpose(ps[:, 6 * BANK + s * P:6 * BANK + (s + 1) * P], w[:, s, :], ident[:, :])
                    last.then_inc(w_used, 1)

            def peer_scores(d):
                l, b = divmod(d, BLOCKS)
                pe.wait_ge(xf_ready, d + 1)
                transposes(0, [xf[b][:, k * P:(k + 1) * P] for k in range(KT)], xfT_ps)
                pe.wait_ge(xfT_ready, d + 1)
                pe.wait_ge(keysT_ready, 2 * l + 2)

                def query(c):
                    for j in range(2):
                        w = half(d, W_QRY0 + c, j, 2 * P)
                        for s in range(2):
                            n = 2 * j + s
                            for k in range(KT):
                                last = pe.matmul(bank(4 + c)[:, n * P:(n + 1) * P], w[:, k, s * P:(s + 1) * P],
                                                 xT[b][:, k, :], start=(k == 0), stop=(k == KT - 1))
                        last.then_inc(w_used, 1)

                def sides(c):
                    pe.wait_ge(qry_ready, ROUTES * d + c + 1)
                    if c >= 2:
                        pe.wait_ge(side_ready, ROUTES * d + c - 1)
                    for s in range(4):
                        last = pe.matmul(bank(c % 2)[:, s * P:(s + 1) * P], turned[:, 4 * c + s, :],
                                         keysT[:, 4 * c + s, :], start=True, stop=True)
                    last.then_inc(side_ps, 1)

                query(0)
                for c in range(1, ROUTES):
                    query(c)
                    sides(c - 1)
                sides(ROUTES - 1)

            pe.wait_ge(consts, 4)
            xm_transposes(0)
            project_in(0, (Q, KV))
            xm_transposes(1)
            project_in(0, (ZU, ZV))
            qk_transposes(0)
            project_in(0, (GA0, GA1))
            scores(0)
            project_in(0, (GB0, GB1))
            spatial(0)
            probs_transposes(0)
            project_in(1, (Q,))
            probs_values(0)
            project_in(1, (KV,))
            gmlp_branch(0)
            attn_branch(0)
            project_in(1, (ZU,))
            project_out(0)
            project_in(1, (ZV,))
            key_transposes(0)
            peer_scores(0)

            project_in(1, (GA0, GA1, GB0, GB1))
            for d in range(1, STEPS):
                if d > 1:
                    xm_transposes(d)
                    project_in(d, range(Q, GB1 + 1))
                qk_transposes(d)
                scores(d)
                spatial(d)
                probs_transposes(d)
                probs_values(d)
                gmlp_branch(d)
                attn_branch(d)
                project_out(d)
                if d % BLOCKS == 0:
                    key_transposes(d)
                peer_scores(d)

        @block_ctx.scalar
        def _(act):
            def used(d, c):
                act.wait_ge(w_used, halves_used(d, c))

            roots = [0]

            def root():
                roots[0] += 1
                act.wait_ge(sq_in, roots[0])
                act.activation(stat[:, 1:2], stat[:, 0:1], ACT.Sqrt).then_inc(sq_out, 1)

            def take_xm(d):
                l, b = divmod(d, BLOCKS)
                act.wait_ge(xmT_ps, d + 1)
                act.activation(xT[b][:, :, :], ps[:, 0:DM].rearrange("p (k n) -> p k n", k=KT), ACT.Copy)\
                    .then_inc(xmT_ready, 1)
                if b == 0:
                    act.wait_ge(w_spT_ps, l + 1)
                    src = bank(7).rearrange("p (g i) -> p g i", g=GG)
                    act.activation(w_spT[0:CH, :, :], src[0:CH, :, :], ACT.Copy)
                    act.activation(w_spT[CH:P, :, CH:P], src[CH:P, :, CH:P], ACT.Copy).then_inc(w_spT_ready, 1)

            def take_q(d):
                used(d, Q)
                for g in range(NKV):
                    q_g = bank(IN_BANK[d, Q])[:, g * GRP * HD:(g + 1) * GRP * HD].rearrange("p (t d) -> p t d", t=GRP)
                    last = act.activation(qk[:, 0:GRP, g, :], q_g, ACT.Copy)
                last.then_inc(in_out[d % BLOCKS], 1)

            def take_kv(d):
                b = d % BLOCKS
                used(d, KV)
                src = bank(IN_BANK[d, KV], 2 * P).rearrange("p (s g d) -> p s g d", s=2, g=NKV)
                act.activation(qk[:, 4, :, :], src[:, 0, :, :], ACT.Copy)
                act.activation(v_tok[b][:, :, :], src[:, 1, :, :], ACT.Copy).then_inc(in_out[b], 1)

            def take_z(d, c):
                used(d, c)
                if d > 0:
                    act.wait_ge(spat_ready, d)
                act.activation((gu if c == ZU else gv)[:, :], bank(IN_BANK[d, c]), ACT.Gelu)\
                    .then_inc(in_out[d % BLOCKS], 1)

            def take_gates(d, chunks):
                if d > 0:
                    act.wait_ge(mergedT_ps, d)
                for c in chunks:
                    used(d, c)
                    k = c - GA0
                    act.activation(sig[:, k // 2, (k % 2) * BANK:(k % 2 + 1) * BANK], bank(IN_BANK[d, c]), ACT.Sigmoid)\
                        .then_inc(in_out[d % BLOCKS], 1)

            def take_qkT(d):
                b = d % BLOCKS
                act.wait_ge(qkT_ps, d + 1)
                act.activation(qT[:, :, :], bank(0).rearrange("p (t n) -> p t n", t=GRP), ACT.Copy)
                act.activation(kT[b][:, :], bank(1, P), ACT.Copy).then_inc(qkT_ready, 1)

            def exps(d):
                b = d % BLOCKS
                act.wait_ge(att_max, d + 1)
                act.activation(att_m[:, 1, :], att_m[:, 1, :], ACT.Exp)
                for hh in range(NH):
                    row = probs[:, hh, 1 - b:2, :].rearrange("p s k -> p (s k)")
                    last = act.activation(row, row, ACT.Exp, bias=att_m[:, 0, hh:hh + 1],
                                          accum_out=att_m[:, 2, hh:hh + 1])
                last.then_inc(att_exp, 1)

            def take_probsT(d):
                b = d % BLOCKS
                act.wait_ge(probsT_ps, d + 1)
                src = att_psum(b)
                dst = turned[:, :, :].rearrange("p (h s) k -> p h s k", s=2)[:, :, 1 - b:2, :]
                for n in range(4):
                    last = act.activation(dst[:, 2 * n:2 * n + 2, :, :], src[:, 2 * n:2 * n + 2, :, :], ACT.Copy)
                last.then_inc(probsT_ready, 1)

            def take_spatT(d):
                act.wait_ge(branchT_ps, 2 * d + 1)
                act.activation(spatT[:, :, :], bank(1).rearrange("p (t n) -> p t n", t=4), ACT.Copy)\
                    .then_inc(branchT_ready, 1)

            def take_attnT(d):
                act.wait_ge(branchT_ps, 2 * d + 2)
                act.activation(attnT[:, :, :], bank(0).rearrange("p (t n) -> p t n", t=4), ACT.Copy)\
                    .then_inc(branchT_ready, 1)

            def take_mergedT(d):
                act.wait_ge(mergedT_ps, d + 1)
                act.activation(xT[d % BLOCKS][:, :, :], ps[:, 0:DM].rearrange("p (k n) -> p k n", k=KT), ACT.Copy)\
                    .then_inc(mergedT_ready, 1)

            def take_keysT(d):
                for half in range(2):
                    act.wait_ge(w_used, halves_used(d, KEYS) - 1 + half)
                    act.activation(keysT[:, half * 8:half * 8 + 8, :],
                                   ps[:, 6 * BANK:8 * BANK].rearrange("p (s k) -> p s k", s=8), ACT.Copy)\
                        .then_inc(keysT_ready, 1)

            def take_xfT(d):
                act.wait_ge(xfT_ps, d + 1)
                act.activation(xT[d % BLOCKS][:, :, :], ps[:, 0:DM].rearrange("p (k n) -> p k n", k=KT), ACT.Copy)\
                    .then_inc(xfT_ready, 1)

            def take_query(d, c):
                used(d, W_QRY0 + c)
                act.activation(turned[:, 4 * c:4 * c + 4, :], bank(4 + c).rearrange("p (s n) -> p s n", s=4),
                               ACT.Copy).then_inc(qry_ready, 1)

            def take_sides(d, c):
                act.wait_ge(side_ps, ROUTES * d + c + 1)
                act.activation(side_scores[:, 4 * c:4 * c + 4, :], bank(c % 2).rearrange("p (s n) -> p s n", s=4),
                               ACT.Copy).then_inc(side_ready, 1)

            def take_peer(d):
                take_xfT(d)
                take_query(d, 0)
                for c in range(1, ROUTES):
                    take_query(d, c)
                    take_sides(d, c - 1)
                take_sides(d, ROUTES - 1)

            def gate_exps(d, r):
                act.wait_ge(gate_args, ROUTES * d + r + 1)
                pairs = pair_s[:, r * R_HEADS:(r + 1) * R_HEADS, :]
                act.activation(pairs, pairs, ACT.Exp).then_inc(gate_exp, 1)

            def gelus(e, first, last):
                with act.Fori(first, last) as w:
                    act.wait_ge(u_used, w * UNIT + (e * PICKS + UNIT))
                    act.activation(acts[:, bass.ds(w * UNIT, UNIT)], dots[:, bass.ds(w * UNIT, UNIT)], ACT.Gelu)\
                        .then_inc(gelu_done, 1)

            act.wait_ge(rope_args, 1)
            act.activation(sin[:, :, :], ang[:, :, :], ACT.Sin)
            act.activation(cos[:, :, :], turn_n[:, :, :], ACT.Sin).then_inc(rope_tab, 1)

            root()
            take_xm(0)
            root()
            take_q(0)
            take_kv(0)
            take_xm(1)
            take_z(0, ZU)
            take_z(0, ZV)
            root()
            take_qkT(0)
            take_gates(0, (GA0, GA1))
            exps(0)
            take_gates(0, (GB0, GB1))
            take_probsT(0)
            take_q(1)
            take_kv(1)
            take_spatT(0)
            take_attnT(0)
            take_z(1, ZU)
            take_mergedT(0)
            take_z(1, ZV)
            root()
            take_keysT(0)
            take_peer(0)
            gate_exps(0, 0)

            for e in range(STEPS - 1):
                d = e + 1
                if d == 1:
                    take_gates(1, (GA0, GA1, GB0, GB1))
                else:
                    root()
                    take_xm(d)
                gelus(e, 0, 2)
                gate_exps(e, 1)
                if d > 1:
                    take_q(d)
                    take_kv(d)
                gelus(e, 2, 4)
                gate_exps(e, 2)
                if d > 1:
                    take_z(d, ZU)
                    take_z(d, ZV)
                gelus(e, 4, 6)
                gate_exps(e, 3)
                if d > 1:
                    take_gates(d, (GA0, GA1))
                take_qkT(d)
                if d > 1:
                    take_gates(d, (GB0, GB1))
                gelus(e, 6, 7)
                root()
                exps(d)
                gelus(e, 7, 8)
                take_probsT(d)
                gelus(e, 8, 9)
                take_spatT(d)
                gelus(e, 9, 10)
                take_attnT(d)
                gelus(e, 10, 11)
                take_mergedT(d)
                gelus(e, 11, 12)
                if d % BLOCKS == 0:
                    take_keysT(d)
                root()
                take_xfT(d)
                take_query(d, 0)
                gelus(e, 12, 13)
                take_query(d, 1)
                take_sides(d, 0)
                for c in range(2, ROUTES):
                    take_query(d, c)
                    take_sides(d, c - 1)
                take_sides(d, ROUTES - 1)
                gelus(e, 13, 14)
                gate_exps(d, 0)
                gelus(e, 14, 16)

            e = STEPS - 1
            for r in range(1, ROUTES):
                gelus(e, 2 * r - 2, 2 * r)
                gate_exps(e, r)
            gelus(e, 6, 7)
            root()
            gelus(e, 7, UNITS)
            root()

        @block_ctx.vector
        def _(vec):
            links = [0]

            def link(ins):
                links[0] += 1
                ins.then_inc(dve, 1)
                vec.wait_ge(dve, links[0])

            roots = [0]

            def rsqrt_of_stat():
                roots[0] += 1
                vec.wait_ge(sq_out, roots[0])
                link(vec.reciprocal(stat[:, 2:3], stat[:, 1:2]))
                link(vec.scalar_tensor_tensor(out=stat[:, 4:5], in0=stat[:, 2:3], scalar=stat[:, 2:3],
                                              in1=stat[:, 0:1], op0=ALU.mult, op1=ALU.mult))
                link(vec.tensor_scalar(stat[:, 4:5], stat[:, 4:5], -0.5, 1.5, ALU.mult, ALU.add))
                link(vec.tensor_tensor(stat[:, 3:4], stat[:, 2:3], stat[:, 4:5], ALU.mult))

            def mean_square(src, spare, width):
                link(vec.scalar_tensor_tensor(out=spare, in0=src, scalar=1.0, in1=src, op0=ALU.mult, op1=ALU.mult,
                                              accum_out=stat[:, 5:6]))
                vec.tensor_scalar(stat[:, 0:1], stat[:, 5:6], 1.0 / width, EPS, ALU.mult, ALU.add).then_inc(sq_in, 1)

            def norm_begin(src):
                mean_square(src[:, :], junk[:, :], DM)

            def norm_end(src, dst, gain, ready):
                rsqrt_of_stat()
                vec.scalar_tensor_tensor(out=dst[:, :], in0=src[:, :], scalar=stat[:, 3:4], in1=gain[:, :],
                                         op0=ALU.mult, op1=ALU.mult).then_inc(ready, 1)

            def rope_tables():
                vec.memset(w_spT[CH:P, :, 0:CH], 0.0)
                for j in range(HALF):
                    last = vec.memset(inv_freq[:, j:j + 1], float(np.float32(THETA ** (-j / HALF))))
                link(last)
                vec.wait_ge(x0_in, 16 * 2)
                for b in range(BLOCKS):
                    link(vec.tensor_copy(stat[:, 6:7], pos[:, b:b + 1]))
                    link(vec.tensor_scalar(ang[:, b, :], inv_freq[:, :], stat[:, 6:7], None, ALU.mult))
                link(vec.tensor_scalar(turn_n[:, :, :], ang[:, :, :], float(1 / (2 * np.pi)), ROUND, ALU.mult, ALU.add))
                link(vec.tensor_scalar(turn_n[:, :, :], turn_n[:, :, :], -ROUND, None, ALU.add))
                for part in two_pi_parts():
                    link(vec.scalar_tensor_tensor(out=ang[:, :, :], in0=turn_n[:, :, :], scalar=-part,
                                                  in1=ang[:, :, :], op0=ALU.mult, op1=ALU.add))
                link(vec.tensor_scalar(ang[:, :, :], ang[:, :, :], PI_DOWN, -PI_DOWN, ALU.min, ALU.max))
                link(vec.tensor_scalar(turn_n[:, :, :], ang[:, :, :], -1.0, None, ALU.mult))
                link(vec.tensor_tensor(turn_n[:, :, :], turn_n[:, :, :], ang[:, :, :], ALU.min))
                vec.tensor_scalar(turn_n[:, :, :], turn_n[:, :, :], float(np.pi / 2), None, ALU.add)\
                    .then_inc(rope_args, 1)

            def rope(d):
                b = d % BLOCKS
                vec.wait_ge(in_out[b], 8 * (d // BLOCKS) + KV + 1)
                if d == 0:
                    vec.wait_ge(rope_tab, 1)
                heads = qk[:, :, :, :].rearrange("p t g d -> p (t g) d")
                lo, hi = heads[:, :, 0:HALF], heads[:, :, HALF:ROT]
                c = cos[:, b, :].unsqueeze(1).to_broadcast([P, 10, HALF])
                s = sin[:, b, :].unsqueeze(1).to_broadcast([P, 10, HALF])
                vec.tensor_tensor(rt[:, 0], lo, c, ALU.mult)
                vec.tensor_tensor(rt[:, 1], hi, s, ALU.mult)
                vec.tensor_tensor(rt[:, 2], hi, c, ALU.mult)
                link(vec.tensor_tensor(rt[:, 3], lo, s, ALU.mult))
                vec.tensor_tensor(lo, rt[:, 0], rt[:, 1], ALU.subtract)
                vec.tensor_tensor(hi, rt[:, 2], rt[:, 3], ALU.add).then_inc(roped, 1)

            def layer_norm_begin(d):
                vec.wait_ge(in_out[d % BLOCKS], 8 * (d // BLOCKS) + ZV + 1)
                if d % BLOCKS == 0:
                    vec.wait_ge(gains_in, 16 * 4 * (d // BLOCKS + 1))
                link(vec.reduce_sum(stat[:, 6:7], gv[:, :], AX))
                link(vec.tensor_scalar(stat[:, 6:7], stat[:, 6:7], -1.0 / GW, None, ALU.mult))
                link(vec.tensor_scalar(gv[:, :], gv[:, :], stat[:, 6:7], None, ALU.add))
                mean_square(gv[:, :], spat[:, :], GW)

            def layer_norm_end(d):
                rsqrt_of_stat()
                link(vec.scalar_tensor_tensor(out=gv[:, :], in0=gv[:, :], scalar=stat[:, 3:4], in1=ln_g[:, :],
                                              op0=ALU.mult, op1=ALU.mult))
                vec.tensor_tensor(gv[:, :], gv[:, :], ln_b[:, :], ALU.add).then_inc(ln_ready, 1)

            def softmax_args(d):
                l, b = divmod(d, BLOCKS)
                if d == 0:
                    vec.wait_ge(consts, 7)
                    vec.wait_ge(small_in, 16 * 3)
                vec.wait_ge(att_ps, d + 1)
                cols = (1 + b) * P
                src = att_psum(b).rearrange("p h s k -> p h (s k)")
                dst = probs[:, :, :, :].rearrange("p h s k -> p h (s k)")[:, :, 2 * P - cols:2 * P]
                m = mask[:, :, :].rearrange("p s k -> p (s k)")[:, 2 * P - cols:2 * P]
                m = m.unsqueeze(1).to_broadcast([P, NH, cols])
                link(vec.scalar_tensor_tensor(out=dst, in0=src, scalar=float(HD ** -0.5), in1=m,
                                              op0=ALU.mult, op1=ALU.add))
                link(vec.tensor_reduce(att_m[:, 0, :], dst, AX, ALU.max))
                link(vec.tensor_tensor(att_m[:, 0, :], att_m[:, 0, :], sinks[:, l, :], ALU.max))
                link(vec.tensor_tensor(att_m[:, 1, :], sinks[:, l, :], att_m[:, 0, :], ALU.subtract))
                vec.tensor_scalar(att_m[:, 0, :], att_m[:, 0, :], -1.0, None, ALU.mult).then_inc(att_max, 1)

            def spatial_gate(d):
                l = d // BLOCKS
                vec.wait_ge(spat_ps, d + 1)
                for g in range(GG):
                    last = vec.scalar_tensor_tensor(
                        out=spat[:, g * GD:(g + 1) * GD], in0=ps[:, BANK + g * GD:BANK + (g + 1) * GD],
                        scalar=b_sp[:, l, g:g + 1], in1=gu[:, g * GD:(g + 1) * GD], op0=ALU.add, op1=ALU.mult)
                last.then_inc(spat_ready, 1)

            def attention_out(d):
                vec.wait_ge(pv_ps, d + 1)
                link(vec.tensor_tensor(att_m[:, 3, :], att_m[:, 2, :], att_m[:, 1, :], ALU.add))
                link(vec.reciprocal(att_m[:, 3, :], att_m[:, 3, :]))
                vec.tensor_tensor(attn[:, :, :], bank(0).rearrange("p (h d) -> p h d", h=NH),
                                  att_m[:, 3, :].unsqueeze(2).to_broadcast([P, NH, HD]), ALU.mult)\
                    .then_inc(attn_ready, 1)

            def merge(d):
                vec.wait_ge(w_used, halves_used(d, W_ATTN))
                vec.tensor_tensor(sig[:, 0, :], sig[:, 0, :], ps[:, 4 * BANK:6 * BANK], ALU.mult)
                link(vec.tensor_tensor(sig[:, 1, :], sig[:, 1, :], ps[:, 6 * BANK:8 * BANK], ALU.mult))
                vec.tensor_tensor(sig[:, 0, :], sig[:, 0, :], sig[:, 1, :], ALU.add).then_inc(merged, 1)

            def add_mixer(d):
                b = d % BLOCKS
                vec.wait_ge(w_used, halves_used(d, W_OUT1))
                link(vec.tensor_tensor(h[b][:, :], h[b][:, :], ps[:, 4 * BANK:6 * BANK], ALU.add))
                norm_begin(h[b])
                norm_end(h[b], xf[b], gain_ffn, xf_ready)

            def top16(scores, values, indices):
                link(vec.max(values[:, 0:8], scores))
                vec.max_index(indices[:, 0:8], values[:, 0:8], scores)
                link(vec.match_replace(scores, values[:, 0:8], scores, LOWEST))
                link(vec.max(values[:, 8:16], scores))
                return vec.max_index(indices[:, 8:16], values[:, 8:16], scores)

            def side_top(d, r):
                vec.wait_ge(side_ready, ROUTES * d + r + 1)
                for s in range(r * R_SIDES, (r + 1) * R_SIDES):
                    last = top16(side_scores[:, s, :], top_v[:, s, :], top_i[:, s, :])
                link(last)

            def route(d, r):
                l, b = divmod(d, BLOCKS)
                heads = slice(r * R_HEADS, (r + 1) * R_HEADS)
                picks = slice(r * R_PICKS, (r + 1) * R_PICKS)
                for hh in range(r * R_HEADS, (r + 1) * R_HEADS):
                    c = cand[:, hh % 2, :, :]
                    link(vec.tensor_tensor(c, top_v[:, 2 * hh, :].unsqueeze(2).to_broadcast([P, TOPK, TOPK]),
                                           top_v[:, 2 * hh + 1, :].unsqueeze(1).to_broadcast([P, TOPK, TOPK]), ALU.add))
                    last = top16(c.rearrange("p a b -> p (a b)"), pair_s[:, hh, :],
                                 pair_i[:, hh * TOPK:(hh + 1) * TOPK])
                link(last)
                link(vec.tensor_copy(gsum[:, heads], pair_s[:, heads, 0]))
                vec.tensor_tensor(pair_s[:, heads, :], pair_s[:, heads, :],
                                  gsum[:, heads].unsqueeze(2).to_broadcast([P, R_HEADS, TOPK]), ALU.subtract)\
                    .then_inc(gate_args, 1)
                vec.tensor_single_scalar(pair_ab[:, 0, picks], pair_i[:, picks], 4, ALU.logical_shift_right)
                link(vec.tensor_single_scalar(pair_ab[:, 1, picks], pair_i[:, picks], TOPK - 1, ALU.bitwise_and))
                for side in range(2):
                    last = vec.tensor_tensor(one_hot[:, side, :, :],
                                             pair_ab[:, side, picks].unsqueeze(2).to_broadcast([P, R_PICKS, TOPK]),
                                             iota[:, :].unsqueeze(1).to_broadcast([P, R_PICKS, TOPK]), ALU.is_equal)
                link(last)
                for side in range(2):
                    per_head = one_hot[:, side, :, :].rearrange("p (h j) m -> p h j m", h=R_HEADS)
                    places = top_i[:, :, :].rearrange("p (h t) m -> p h t m", t=2)[:, heads, side, :]
                    last = vec.tensor_tensor(per_head, per_head,
                                             places.unsqueeze(2).to_broadcast([P, R_HEADS, TOPK, TOPK]), ALU.mult)
                link(last)
                link(vec.tensor_reduce(key_ab[:, 0:2, picks], one_hot[:, :, :, :], AX, ALU.add))
                link(vec.scalar_tensor_tensor(out=key_ab[:, 2, picks], in0=key_ab[:, 0, picks], scalar=float(NK),
                                              in1=key_ab[:, 1, picks], op0=ALU.mult, op1=ALU.add))
                vec.tensor_scalar(ids[b][:, picks], key_ab[:, 2, picks], float(l * NE), None, ALU.add)\
                    .then_inc(routed, 1)
                vec.wait_ge(gate_exp, ROUTES * d + r + 1)
                link(vec.reduce_sum(gsum[:, heads], pair_s[:, heads, :], AX))
                link(vec.reciprocal(gsum[:, heads], gsum[:, heads]))
                vec.tensor_tensor(gates[b][:, picks].rearrange("p (h j) -> p h j", h=R_HEADS), pair_s[:, heads, :],
                                  gsum[:, heads].unsqueeze(2).to_broadcast([P, R_HEADS, TOPK]), ALU.mult)\
                    .then_inc(routed, 1)

            def u_pick(e, w, i):
                vec.wait_ge(u_landed[i % RING], w * (16 * TURNS) + 16 * (e * UNITS * TURNS + i // RING + 1))
                vec.scalar_tensor_tensor(out=junk[:, :], in0=xf[e % BLOCKS][:, :], scalar=1.0,
                                         in1=u_ring[:, i % RING, :], op0=ALU.mult, op1=ALU.mult,
                                         accum_out=dots[:, bass.ds(w * UNIT + i, 1)]).then_inc(u_used, 1)

            def coefficients(e, w):
                cols = bass.ds(w * UNIT - LAG * UNIT, UNIT)
                vec.wait_ge(gelu_done, w + (e * UNITS - LAG + 1))
                vec.tensor_tensor(coef[:, cols], acts[:, cols], gates[e % BLOCKS][:, cols], ALU.mult)\
                    .then_inc(coef_ready, 1)
                vec.wait_ge(coef_ready, w + (e * UNITS - LAG + 1))

            def v_pick(e, w, i):
                hb = h[e % BLOCKS]
                vec.wait_ge(v_landed[i % RING], w * (16 * TURNS) + 16 * ((e * UNITS - LAG) * TURNS + i // RING + 1))
                vec.scalar_tensor_tensor(out=hb[:, :], in0=v_ring[:, i % RING, :],
                                         scalar=coef[:, bass.ds(w * UNIT + (i - LAG * UNIT), 1)],
                                         in1=hb[:, :], op0=ALU.mult, op1=ALU.add).then_inc(v_used, 1)

            def units(e, first, last):
                with vec.Fori(first, last) as w:
                    if first >= LAG:
                        coefficients(e, w)
                    for i in range(UNIT):
                        if last <= UNITS:
                            u_pick(e, w, i)
                        if first >= LAG:
                            if i > 0:
                                vec.wait_ge(v_used, w * UNIT + (e * PICKS - LAG * UNIT + i))
                            v_pick(e, w, i)
                        if last <= UNITS:
                            vec.wait_ge(u_used, w * UNIT + (e * PICKS + i + 1))
                    if first >= LAG:
                        vec.wait_ge(v_used, w * UNIT + (e * PICKS - LAG * UNIT + UNIT))

            def first_units(e):
                for r in range(1, ROUTES):
                    units(e, 2 * r - 2, 2 * r - 1)
                    side_top(e, r)
                    units(e, 2 * r - 1, 2 * r)
                    route(e, r)

            rope_tables()
            norm_begin(h[0])
            vec.wait_ge(mix_in, 16)
            norm_end(h[0], xf[0], gain_mix, xm_ready)
            vec.wait_ge(x1_in, 16)
            norm_begin(h[1])
            norm_end(h[1], xf[1], gain_mix, xm_ready)
            rope(0)
            layer_norm_begin(0)
            layer_norm_end(0)
            softmax_args(0)
            spatial_gate(0)
            attention_out(0)
            merge(0)
            add_mixer(0)
            side_top(0, 0)
            route(0, 0)

            for e in range(STEPS - 1):
                d, b = e + 1, (e + 1) % BLOCKS
                if d > 1:
                    norm_begin(h[b])
                    vec.wait_ge(mix_in, 16 * 2)
                    norm_end(h[b], xf[b], gain_mix, xm_ready)
                first_units(e)
                rope(d)
                units(e, 6, 7)
                layer_norm_begin(d)
                layer_norm_end(d)
                softmax_args(d)
                units(e, 7, 8)
                spatial_gate(d)
                units(e, 8, 9)
                attention_out(d)
                units(e, 9, 10)
                merge(d)
                units(e, 10, 12)
                add_mixer(d)
                units(e, 12, 13)
                side_top(d, 0)
                units(e, 13, 14)
                route(d, 0)
                units(e, 14, UNITS)
                units(e, UNITS, UNITS + LAG)

            e = STEPS - 1
            first_units(e)
            units(e, 6, 7)
            norm_begin(h[0])
            vec.wait_ge(mix_in, 16 * 3)
            norm_end(h[0], xf[0], gain_mix, y_ready)
            units(e, 7, UNITS)
            units(e, UNITS, UNITS + LAG)
            norm_begin(h[1])
            norm_end(h[1], xf[1], gain_mix, y_ready)


_INS = ["x", "positions", "norm_mix_g", "w_in", "attn_sinks", "gmlp_ln_g", "gmlp_ln_b", "w_spatial", "b_spatial",
        "w_attn_branch", "w_gmlp_branch", "w_out", "norm_ffn_g", "peer_w_query", "peer_sub_keys", "peer_u", "peer_v",
        "final_norm_g"]


def kernel(**inputs):
    import concourse.bacc as _bacc
    from concourse.bass_utils import run_bass_kernel_spmd as _run

    nc = _bacc.Bacc("TRN2", target_bir_lowering=False, num_devices=1)
    arrays, args = {}, []
    for name in _INS:
        a = np.ascontiguousarray(inputs[name])
        arrays[f"in_{name}"] = a
        args.append(nc.dram_tensor(f"in_{name}", a.shape, mybir.dt.from_np(a.dtype), kind="ExternalInput").ap())
    args.append(nc.dram_tensor("out_trunk", (1, BLOCKS * P, DM), F32, kind="ExternalOutput").ap())
    build(nc, *args)
    r = _run(nc, [arrays], core_ids=[0])
    return r.results[0]["out_trunk"]
```

```python
from contextlib import ExitStack

import numpy as np

import concourse.bass as bass
from concourse import mybir

F32 = mybir.dt.float32
I32 = mybir.dt.int32
U32 = mybir.dt.uint32
ALU = mybir.AluOpType
ACT = mybir.ActivationFunctionType
AX = mybir.AxisListType.X

P = 128
BLOCKS = 2
DM = 1024
KT = DM // P
DEPTH = 2
STEPS = DEPTH * BLOCKS
CH = 64
NH, NKV, HD = 8, 2, 64
GRP = NH // NKV
ROT = HD // 4
HALF = ROT // 2
THETA = 500000.0
GW, GG = 512, 4
GD = GW // GG
PH, NK, KD = 8, 128, 128
SIDES = 2 * PH
NE = NK * NK
TOPK = 16
PICKS = PH * TOPK
EPS = 1e-6
MASKED = -1e30
LOWEST = -3.0e38
BANK = 512

UNIT = 8
UNITS = PICKS // UNIT
LAG = 2
RING = 8
TURNS = UNIT // RING
WSLOTS = 4

PI_DOWN = float(np.nextafter(np.float32(np.pi), np.float32(0)))
ROUND = float(1.5 * 2 ** 23)


def two_pi_parts():
    rest, parts = 2 * np.pi, []
    for _ in range(3):
        scale = 2.0 ** (np.floor(np.log2(rest)) - 7)
        parts.append(float(np.floor(rest / scale) * scale))
        rest -= parts[-1]
    return parts + [float(rest)]


IN_COLS = [(0, 512), (512, 256), (768, 512), (1280, 512), (1792, 512), (2304, 512), (2816, 512), (3328, 512)]
Q, KV, ZU, ZV, GA0, GA1, GB0, GB1, W_ATTN, W_GMLP, W_OUT0, W_OUT1, W_QRY0 = range(13)
KEYS = W_QRY0 + 4
ROUTES = 4
R_HEADS = PH // ROUTES
R_SIDES = SIDES // ROUTES
R_PICKS = PICKS // ROUTES


def chunk_order():
    dense = [Q, KV, ZU, ZV, GA0, GA1, GB0, GB1]
    tail = [W_GMLP, W_ATTN, W_OUT0, W_OUT1]
    query = [W_QRY0 + c for c in range(4)]
    order = [(0, c) for c in dense] + [(1, Q), (1, KV), (0, W_GMLP), (0, W_ATTN), (1, ZU), (0, W_OUT0), (0, W_OUT1),
                                       (1, ZV), (0, KEYS)] + [(0, c) for c in query]
    order += [(1, c) for c in [GA0, GA1, GB0, GB1] + tail + query]
    order += [(2, c) for c in dense + tail + [KEYS] + query]
    order += [(3, c) for c in dense + tail + query]
    return order


ORDER = chunk_order()
NUMBER = {dc: n for n, dc in enumerate(ORDER)}
IN_ORDER = [dc for dc in ORDER if dc[1] <= GB1]
IN_BANK = {dc: 2 + n % 2 for n, dc in enumerate(IN_ORDER)}
IN_BEFORE = {dc: IN_ORDER[n - 2] for n, dc in enumerate(IN_ORDER) if n >= 2}


EARLY = [2 * NUMBER[1, c] + j for c in (GA0, GA1) for j in range(2)]
EARLY_AFTER = {(0, KV): 0, (0, ZU): 1, (0, GB1): 2, (0, W_ATTN): 3}
assert len(EARLY) == WSLOTS and EARLY[-1] == EARLY[0] + WSLOTS - 1


def halves_used(d, c):
    return 2 * NUMBER[d, c] + 2


def build(nc, x, positions, norm_mix_g, w_in, attn_sinks, gmlp_ln_g, gmlp_ln_b, w_spatial, b_spatial,
          w_attn_branch, w_gmlp_branch, w_out, norm_ffn_g, peer_w_query, peer_sub_keys, peer_u, peer_v,
          final_norm_g, out):
    u_rows = peer_u.rearrange("l e d -> (l e) d")
    v_rows = peer_v.rearrange("l e d -> (l e) d")

    with ExitStack() as ctx:
        def sb(name, shape, dt=F32):
            return ctx.enter_context(nc.sbuf_tensor(name, shape, dt))

        def sem(name):
            return ctx.enter_context(nc.semaphore(name))

        h = [sb(f"h{b}", [P, DM]) for b in range(BLOCKS)]
        xf = [sb(f"xf{b}", [P, DM]) for b in range(BLOCKS)]
        xT = [sb(f"xT{b}", [P, KT, P]) for b in range(BLOCKS)]
        qk = sb("qk", [P, 5, 2, HD])
        v_tok = [sb(f"v_tok{b}", [P, NKV, HD]) for b in range(BLOCKS)]
        qT = sb("qT", [P, GRP, P])
        kT = [sb(f"kT{b}", [P, P]) for b in range(BLOCKS)]
        gu = sb("gu", [P, GW])
        gv = sb("gv", [P, GW])
        spatT = gu[:, :].rearrange("p (t n) -> p t n", t=4)
        attnT = gv[:, :].rearrange("p (t n) -> p t n", t=4)
        sig = sb("sig", [P, 2, DM])
        probs = sb("probs", [P, NH, 2, P])
        side_scores = probs[:, :, :, :].rearrange("p h s k -> p (h s) k")
        turned = sb("turned", [P, SIDES, P])
        attn = sb("attn", [P, NH, HD])
        spat = sb("spat", [P, GW])
        rt = sb("rt", [P, 4, 10, HALF])
        keysT = sb("keysT", [P, SIDES, NK])
        w_sp = sb("w_sp", [P, GG, P])
        w_spT = sb("w_spT", [P, GG, P])
        gain_mix = sb("gain_mix", [P, DM])
        gain_ffn = sb("gain_ffn", [P, DM])
        ln_g = sb("ln_g", [P, GW])
        ln_b = sb("ln_b", [P, GW])
        b_sp = sb("b_sp", [P, DEPTH, GG])
        sinks = sb("sinks", [P, DEPTH, NH])
        mask = sb("mask", [P, 2, P])
        ident = sb("ident", [P, P])
        pos = sb("pos", [P, BLOCKS], I32)
        inv_freq = sb("inv_freq", [P, HALF])
        ang = sb("ang", [P, BLOCKS, HALF])
        turn_n = sb("turn_n", [P, BLOCKS, HALF])
        cos = sb("cos", [P, BLOCKS, HALF])
        sin = sb("sin", [P, BLOCKS, HALF])
        iota = sb("iota", [P, TOPK])
        stat = sb("stat", [P, 8])
        att_m = sb("att_m", [P, 4, NH])
        top_v = sb("top_v", [P, SIDES, TOPK])
        top_i = sb("top_i", [P, SIDES, TOPK], U32)
        cand = sb("cand", [P, 2, TOPK, TOPK])
        pair_s = sb("pair_s", [P, PH, TOPK])
        pair_i = sb("pair_i", [P, PICKS], U32)
        pair_ab = sb("pair_ab", [P, 2, PICKS], U32)
        one_hot = sb("one_hot", [P, 2, R_PICKS, TOPK])
        key_ab = sb("key_ab", [P, 3, PICKS])
        gsum = sb("gsum", [P, PH])
        gates = [sb(f"gates{b}", [P, PICKS]) for b in range(BLOCKS)]
        ids = sb("ids", [P, STEPS * PICKS], I32)
        dots = sb("dots", [P, PICKS])
        acts = sb("acts", [P, PICKS])
        coef = sb("coef", [P, PICKS])
        junk = sb("junk", [P, DM])
        staged = sb("staged", [P, 2, 2, UNIT], I32)
        u_ring = sb("u_ring", [P, RING, DM])
        v_ring = sb("v_ring", [P, RING, DM])
        w_ring = sb("w_ring", [P, WSLOTS, KT * BANK // 2])
        ps = ctx.enter_context(nc.psum_tensor("ps", [P, 8 * BANK], F32))

        def bank(n, width=BANK):
            return ps[:, n * BANK:n * BANK + width]

        def early_buf(i):
            return v_ring[:, 2 * i:2 * i + 2, :].rearrange("p r (k n) -> p (r k) n", n=BANK)

        def att_psum(b):
            return ps[:, 4 * BANK:4 * BANK + NH * (1 + b) * P].rearrange("p (h s k) -> p h s k", h=NH, s=1 + b)

        x0_in = sem("x0_in")
        x1_in = sem("x1_in")
        small_in = sem("small_in")
        mix_in = sem("mix_in")
        gains_in = sem("gains_in")
        w_landed = [sem(f"w_landed{s}") for s in range(WSLOTS)]
        early_landed = [sem(f"early_landed{j}") for j in range(len(EARLY))]
        w_used = sem("w_used")
        out_done = sem("out_done")
        consts = sem("consts")
        rope_args = sem("rope_args")
        rope_tab = sem("rope_tab")
        dve = sem("dve")
        sq_in = sem("sq_in")
        sq_out = sem("sq_out")
        xm_ready = sem("xm_ready")
        xmT_ps = sem("xmT_ps")
        xmT_ready = sem("xmT_ready")
        w_spT_ps = sem("w_spT_ps")
        w_spT_ready = sem("w_spT_ready")
        in_out = [sem(f"in_out{b}") for b in range(BLOCKS)]
        roped = sem("roped")
        qkT_ps = sem("qkT_ps")
        qkT_ready = sem("qkT_ready")
        att_ps = sem("att_ps")
        att_max = sem("att_max")
        att_exp = sem("att_exp")
        probsT_ps = sem("probsT_ps")
        probsT_ready = sem("probsT_ready")
        pv_ps = sem("pv_ps")
        attn_ready = sem("attn_ready")
        ln_ready = sem("ln_ready")
        spat_ps = sem("spat_ps")
        spat_ready = sem("spat_ready")
        branchT_ps = sem("branchT_ps")
        branchT_ready = sem("branchT_ready")
        merged = sem("merged")
        mergedT_ps = sem("mergedT_ps")
        mergedT_ready = sem("mergedT_ready")
        xf_ready = sem("xf_ready")
        xfT_ps = sem("xfT_ps")
        xfT_ready = sem("xfT_ready")
        keysT_ready = sem("keysT_ready")
        qry_ready = sem("qry_ready")
        side_ps = sem("side_ps")
        side_ready = sem("side_ready")
        gate_args = sem("gate_args")
        gate_exp = sem("gate_exp")
        routed = sem("routed")
        staged_sem = sem("staged")
        u_landed = [sem(f"u_landed{s}") for s in range(RING)]
        v_landed = [sem(f"v_landed{s}") for s in range(RING)]
        u_used = sem("u_used")
        v_used = sem("v_used")
        gelu_done = sem("gelu_done")
        coef_ready = sem("coef_ready")
        y_ready = sem("y_ready")

        block_ctx = ctx.enter_context(nc.Block())

        @block_ctx.sync
        def _(sp):
            def load_layer(l):
                sp.dma_start(w_sp[:, :, :], w_spatial[l].rearrange("g i j -> i g j")).then_inc(gains_in, 16)
                sp.dma_start(ln_g[:, :], gmlp_ln_g[l, :].partition_broadcast(P)).then_inc(gains_in, 16)
                sp.dma_start(ln_b[:, :], gmlp_ln_b[l, :].partition_broadcast(P)).then_inc(gains_in, 16)
                sp.dma_start(gain_ffn[:, :], norm_ffn_g[l, :].partition_broadcast(P)).then_inc(gains_in, 16)

            def load_half(n, cols, src):
                if n >= WSLOTS:
                    sp.wait_ge(w_used, n - WSLOTS + 1)
                dst = w_ring[:, n % WSLOTS, 0:src.shape[1] * cols].rearrange("p (k n) -> p k n", n=cols)
                sp.dma_start(dst, src).then_inc(w_landed[n % WSLOTS], 16)

            def load_early(i):
                d, c = ORDER[EARLY[i] // 2]
                k0 = (EARLY[i] % 2) * DM // 2
                c0, cols = IN_COLS[c]
                sp.dma_start(early_buf(i), w_in[0, k0:k0 + DM // 2, c0:c0 + cols].rearrange("(k p) n -> p k n", p=P))\
                    .then_inc(early_landed[i], 16)

            def load_weights(first, last):
                for n in range(first, last):
                    d, c = ORDER[n]
                    l = d // BLOCKS
                    if n > 0 and ORDER[n - 1] in EARLY_AFTER:
                        load_early(EARLY_AFTER[ORDER[n - 1]])
                    if 2 * n in EARLY:
                        continue
                    for j in range(2):
                        if c <= GB1:
                            c0, cols = IN_COLS[c]
                            w = w_in[l, j * DM // 2:(j + 1) * DM // 2, c0:c0 + cols]
                        elif c in (W_ATTN, W_GMLP):
                            cols = BANK
                            w = (w_attn_branch if c == W_ATTN else w_gmlp_branch)[l, :, j * cols:(j + 1) * cols]
                        elif c in (W_OUT0, W_OUT1):
                            c0, cols = (c - W_OUT0) * BANK, BANK
                            w = w_out[l, j * DM // 2:(j + 1) * DM // 2, c0:c0 + cols]
                        elif c == KEYS:
                            load_half(2 * n + j, KD, peer_sub_keys[l, j * PH // 2:(j + 1) * PH // 2]
                                      .rearrange("h t k d -> k (h t) d"))
                            continue
                        else:
                            cols = BANK // 2
                            c0 = (c - W_QRY0) * BANK + j * cols
                            w = peer_w_query[l, :, c0:c0 + cols]
                        load_half(2 * n + j, cols, w.rearrange("(k p) n -> p k n", p=P))

            sp.dma_start(h[0][:, :], x[0, 0:P, :]).then_inc(x0_in, 16)
            sp.dma_start(pos[:, :], positions[0].rearrange("(b p) -> p b", p=P),
                         allow_slow_non_contiguous=True).then_inc(x0_in, 16)
            sp.dma_start(gain_mix[:, :], norm_mix_g[0, :].partition_broadcast(P)).then_inc(mix_in, 16)
            load_weights(0, 1)
            sp.dma_start(h[1][:, :], x[0, P:2 * P, :]).then_inc(x1_in, 16)
            load_weights(1, 2)
            load_layer(0)
            sp.dma_start(sinks[:, :, :], attn_sinks.partition_broadcast(P)).then_inc(small_in, 16)
            for l in range(DEPTH):
                sp.dma_start(b_sp[:, l, :], b_spatial[l].rearrange("g i -> i g"),
                             allow_slow_non_contiguous=True).then_inc(small_in, 16)
            load_weights(2, NUMBER[2, Q])
            sp.wait_ge(xf_ready, 2)
            sp.dma_start(gain_mix[:, :], norm_mix_g[1, :].partition_broadcast(P)).then_inc(mix_in, 16)
            load_layer(1)
            load_weights(NUMBER[2, Q], len(ORDER))
            sp.wait_ge(xm_ready, 4)
            sp.dma_start(gain_mix[:, :], final_norm_g.partition_broadcast(P)).then_inc(mix_in, 16)
            for b in range(BLOCKS):
                sp.wait_ge(y_ready, b + 1)
                sp.dma_start(out[0, b * P:(b + 1) * P, :], xf[b][:, :]).then_inc(out_done, 16)
            sp.wait_ge(out_done, 16 * BLOCKS)

        @block_ctx.gpsimd
        def _(pool):
            pool.memset(ident[:, :], 0.0).then_inc(consts, 1)
            pool.memset(mask[:, :, :], 0.0).then_inc(consts, 1)
            pool.iota(iota[:, :], [[1, TOPK]], base=0, channel_multiplier=0,
                      allow_small_or_imprecise_dtypes=True).then_inc(consts, 1)
            pool.wait_ge(consts, 3)
            pool.affine_select(out=ident[:, :], in_=ident[:, :], compare_op=ALU.not_equal, fill=1.0, base=0,
                               pattern=[[-1, P]], channel_multiplier=1).then_inc(consts, 1)
            pool.memset(mask[:, 0, 0:CH], MASKED).then_inc(consts, 1)
            pool.wait_ge(consts, 5)
            pool.memset(mask[CH:P, 0, CH:P], MASKED).then_inc(consts, 1)
            pool.wait_ge(consts, 6)
            pool.memset(mask[0:CH, 1, CH:P], MASKED).then_inc(consts, 1)

            def stage(which, unit, parity, count):
                pool.tensor_copy(staged[:, which, parity, :], ids[:, bass.ds(unit * UNIT, UNIT)])\
                    .then_inc(staged_sem, 1)
                pool.wait_ge(staged_sem, count)

            def gather(which, parity, i, turn, first=False):
                table, ring, landed, used = ((u_rows, u_ring, u_landed, u_used),
                                             (v_rows, v_ring, v_landed, v_used))[which]
                if not first:
                    pool.wait_ge(used, turn * RING + i % RING + 1 - RING)
                    pool.nop(nofuse=True)
                pool.indirect_dma_start(
                    out=ring[:, i % RING, :], out_offset=None, in_=table,
                    in_offset=bass.IndirectOffsetOnAxis(ap=staged[:, which, parity, i:i + 1], axis=0),
                ).then_inc(landed[i % RING], 16)

            assert R_HEADS == 2 and TOPK == 2 * UNIT
            all_units = STEPS * UNITS
            pool.wait_ge(routed, 1)
            for w in range(LAG):
                stage(0, w, w % 2, w + 1)
                for i in range(UNIT):
                    gather(0, w % 2, i, w * TURNS, first=w * TURNS + i // RING == 0)
            pool.wait_ge(routed, 2)
            pool.wait_ge(w_used, EARLY[-1] + 1)
            for w in range(LAG, LAG + 2):
                stage(0, w, w % 2, LAG + 2 * (w - LAG) + 1)
                stage(1, w - LAG, w % 2, LAG + 2 * (w - LAG) + 2)
                for i in range(UNIT):
                    gather(0, w % 2, i, w * TURNS)
                    gather(1, w % 2, i, (w - LAG) * TURNS, first=(w - LAG) * TURNS + i // RING == 0)
            with pool.Fori(LAG // 2 + 1, all_units // 2) as pair:
                pool.wait_ge(routed, pair + R_HEADS)
                pool.nop(nofuse=True)
                for s in range(2):
                    stage(0, pair * 2 + s, s, pair * 4 + (LAG - 4 + 2 * s + 1))
                    stage(1, pair * 2 + (s - LAG), s, pair * 4 + (LAG - 4 + 2 * s + 2))
                    for i in range(UNIT):
                        gather(0, s, i, pair * (2 * TURNS) + (s * TURNS + i // RING))
                        gather(1, s, i, pair * (2 * TURNS) + ((s - LAG) * TURNS + i // RING))
            for w in range(all_units, all_units + LAG):
                stage(1, w - LAG, w % 2, 2 * all_units - LAG + (w - all_units) + 1)
                for i in range(UNIT):
                    gather(1, w % 2, i, (w - LAG) * TURNS + i // RING)

        @block_ctx.tensor
        def _(pe):
            def half(d, c, j, cols):
                n = 2 * NUMBER[d, c] + j
                if n in EARLY:
                    pe.wait_ge(early_landed[n - EARLY[0]], 16)
                    return early_buf(n - EARLY[0])
                pe.wait_ge(w_landed[n % WSLOTS], 16 * (n // WSLOTS + (1 if n < EARLY[0] else 0)))
                return w_ring[:, n % WSLOTS, :].rearrange("p (k n) -> p k n", n=cols)

            def project(d, c, dst, lhs, cols):
                for j in range(2):
                    w = half(d, c, j, cols)
                    for k in range(4):
                        last = pe.matmul(dst, lhs[:, 4 * j + k, :], w[:, k, :], start=(j + k == 0),
                                         stop=(j == 1 and k == 3))
                    last.then_inc(w_used, 1)

            def transposes(dst_bank, tiles, done):
                for t, src in enumerate(tiles):
                    last = pe.transpose(ps[:, dst_bank * BANK + t * P:dst_bank * BANK + (t + 1) * P], src, ident[:, :])
                last.then_inc(done, 1)

            def xm_transposes(d):
                b = d % BLOCKS
                pe.wait_ge(xm_ready, d + 1)
                if d == 1:
                    pe.wait_ge(xmT_ready, 1)
                if d >= 2:
                    pe.wait_ge(side_ready, ROUTES * d)
                transposes(0, [xf[b][:, k * P:(k + 1) * P] for k in range(KT)], xmT_ps)

            def w_sp_transposes(d):
                pe.wait_ge(gains_in, 16 * 4 * (d // BLOCKS + 1))
                transposes(7, [w_sp[:, g, :] for g in range(GG)], w_spT_ps)

            def project_in(d, chunks):
                b = d % BLOCKS
                pe.wait_ge(xmT_ready, d + 1)
                for c in chunks:
                    if (d, c) in IN_BEFORE:
                        d0, c0 = IN_BEFORE[d, c]
                        pe.wait_ge(in_out[d0 % BLOCKS], 8 * (d0 // BLOCKS) + c0 + 1)
                    cols = IN_COLS[c][1]
                    project(d, c, bank(IN_BANK[d, c], cols), xT[b], cols)

            def qk_transposes(d):
                pe.wait_ge(roped, d + 1)
                if d == 0:
                    pe.wait_ge(xmT_ready, 2)
                if d == 1:
                    pe.wait_ge(side_ready, ROUTES)
                transposes(0, [qk[:, t, :, :].rearrange("p g d -> p (g d)") for t in range(5)], qkT_ps)

            def scores(d):
                b = d % BLOCKS
                pe.wait_ge(qkT_ready, d + 1)
                if d > 0:
                    pe.wait_ge(qry_ready, ROUTES * d)
                dst = att_psum(b)
                for g in range(NKV):
                    for t in range(GRP):
                        for s in range(1 + b):
                            keys = kT[s]
                            last = pe.matmul(dst[:, g * GRP + t, s, :], qT[g * HD:(g + 1) * HD, t, :],
                                             keys[g * HD:(g + 1) * HD, :], start=True, stop=True)
                last.then_inc(att_ps, 1)

            def spatial(d):
                l, b = divmod(d, BLOCKS)
                pe.wait_ge(ln_ready, d + 1)
                pe.wait_ge(w_spT_ready, l + 1)
                for g in range(GG):
                    last = pe.matmul(bank(1)[:, g * GD:(g + 1) * GD], w_spT[:, g, :],
                                     gv[:, g * GD:(g + 1) * GD], start=True, stop=True)
                last.then_inc(spat_ps, 1)

            def probs_transposes(d):
                b = d % BLOCKS
                pe.wait_ge(att_exp, d + 1)
                dst = att_psum(b)
                for hh in range(NH):
                    for s in range(1 + b):
                        last = pe.transpose(dst[:, hh, s, :], probs[:, hh, 1 - b + s, :], ident[:, :])
                last.then_inc(probsT_ps, 1)

            def probs_values(d):
                b = d % BLOCKS
                pe.wait_ge(probsT_ready, d + 1)
                for hh in range(NH):
                    g = hh // GRP
                    for kb in range(1 - b, 2):
                        vt = v_tok[b] if kb == 1 else v_tok[0]
                        last = pe.matmul(ps[:, hh * HD:(hh + 1) * HD], turned[:, hh * 2 + kb, :], vt[:, g, :],
                                         start=(kb == 1 - b), stop=(kb == 1))
                last.then_inc(pv_ps, 1)

            def branch(d, c, lhs, n_bank):
                for j in range(2):
                    w = half(d, c, j, BANK)
                    for k in range(4):
                        last = pe.matmul(bank(n_bank + j), lhs[:, k, :], w[:, k, :], start=(k == 0), stop=(k == 3))
                    last.then_inc(w_used, 1)

            def gmlp_branch(d):
                pe.wait_ge(spat_ready, d + 1)
                transposes(1, [spat[:, t * P:(t + 1) * P] for t in range(4)], branchT_ps)
                pe.wait_ge(branchT_ready, 2 * d + 1)
                branch(d, W_GMLP, spatT, 6)

            def attn_branch(d):
                pe.wait_ge(attn_ready, d + 1)
                transposes(0, [attn[:, 2 * t:2 * t + 2, :].rearrange("p h d -> p (h d)") for t in range(4)], branchT_ps)
                pe.wait_ge(branchT_ready, 2 * d + 2)
                branch(d, W_ATTN, attnT, 4)

            def project_out(d):
                b = d % BLOCKS
                pe.wait_ge(merged, d + 1)
                transposes(0, [sig[:, 0, k * P:(k + 1) * P] for k in range(KT)], mergedT_ps)
                pe.wait_ge(mergedT_ready, d + 1)
                for n in range(2):
                    project(d, W_OUT0 + n, bank(4 + n), xT[b], BANK)

            def key_transposes(d):
                for j in range(2):
                    if j == 1:
                        pe.wait_ge(keysT_ready, 2 * (d // BLOCKS) + 1)
                    w = half(d, KEYS, j, KD)
                    for s in range(SIDES // 2):
                        last = pe.transpose(ps[:, 6 * BANK + s * P:6 * BANK + (s + 1) * P], w[:, s, :], ident[:, :])
                    last.then_inc(w_used, 1)

            def peer_scores(d):
                l, b = divmod(d, BLOCKS)
                pe.wait_ge(xf_ready, d + 1)
                transposes(0, [xf[b][:, k * P:(k + 1) * P] for k in range(KT)], xfT_ps)
                pe.wait_ge(xfT_ready, d + 1)
                pe.wait_ge(keysT_ready, 2 * l + 2)

                def query(c):
                    for j in range(2):
                        w = half(d, W_QRY0 + c, j, 2 * P)
                        for s in range(2):
                            n = 2 * j + s
                            for k in range(KT):
                                last = pe.matmul(bank(4 + c)[:, n * P:(n + 1) * P], w[:, k, s * P:(s + 1) * P],
                                                 xT[b][:, k, :], start=(k == 0), stop=(k == KT - 1))
                        last.then_inc(w_used, 1)

                def sides(c):
                    pe.wait_ge(qry_ready, ROUTES * d + c + 1)
                    if c >= 2:
                        pe.wait_ge(side_ready, ROUTES * d + c - 1)
                    for s in range(4):
                        last = pe.matmul(bank(c % 2)[:, s * P:(s + 1) * P], turned[:, 4 * c + s, :],
                                         keysT[:, 4 * c + s, :], start=True, stop=True)
                    last.then_inc(side_ps, 1)

                query(0)
                sides(0)
                query(1)
                for c in range(2, ROUTES):
                    query(c)
                    sides(c - 1)
                sides(ROUTES - 1)

            pe.wait_ge(consts, 4)
            xm_transposes(0)
            project_in(0, (Q, KV))
            xm_transposes(1)
            project_in(0, (ZU, ZV))
            qk_transposes(0)
            w_sp_transposes(0)
            project_in(0, (GA0, GA1))
            scores(0)
            project_in(0, (GB0, GB1))
            spatial(0)
            probs_transposes(0)
            project_in(1, (Q,))
            probs_values(0)
            project_in(1, (KV,))
            gmlp_branch(0)
            attn_branch(0)
            project_in(1, (ZU,))
            project_out(0)
            project_in(1, (ZV,))
            key_transposes(0)
            peer_scores(0)

            project_in(1, (GA0, GA1, GB0, GB1))
            for d in range(1, STEPS):
                if d > 1:
                    xm_transposes(d)
                    project_in(d, range(Q, GB1 + 1))
                qk_transposes(d)
                if d > 1 and d % BLOCKS == 0:
                    w_sp_transposes(d)
                scores(d)
                spatial(d)
                probs_transposes(d)
                probs_values(d)
                gmlp_branch(d)
                attn_branch(d)
                project_out(d)
                if d % BLOCKS == 0:
                    key_transposes(d)
                peer_scores(d)

        @block_ctx.scalar
        def _(act):
            def used(d, c):
                act.wait_ge(w_used, halves_used(d, c))

            roots = [0]

            def root():
                roots[0] += 1
                act.wait_ge(sq_in, roots[0])
                act.activation(stat[:, 1:2], stat[:, 0:1], ACT.Sqrt).then_inc(sq_out, 1)

            def take_xm(d):
                b = d % BLOCKS
                act.wait_ge(xmT_ps, d + 1)
                act.activation(xT[b][:, :, :], ps[:, 0:DM].rearrange("p (k n) -> p k n", k=KT), ACT.Copy)\
                    .then_inc(xmT_ready, 1)

            def take_w_spT(d):
                act.wait_ge(w_spT_ps, d // BLOCKS + 1)
                src = bank(7).rearrange("p (g i) -> p g i", g=GG)
                act.activation(w_spT[0:CH, :, :], src[0:CH, :, :], ACT.Copy)
                act.activation(w_spT[CH:P, :, CH:P], src[CH:P, :, CH:P], ACT.Copy).then_inc(w_spT_ready, 1)

            def take_q(d):
                used(d, Q)
                for g in range(NKV):
                    q_g = bank(IN_BANK[d, Q])[:, g * GRP * HD:(g + 1) * GRP * HD].rearrange("p (t d) -> p t d", t=GRP)
                    last = act.activation(qk[:, 0:GRP, g, :], q_g, ACT.Copy)
                last.then_inc(in_out[d % BLOCKS], 1)

            def take_kv(d):
                b = d % BLOCKS
                used(d, KV)
                src = bank(IN_BANK[d, KV], 2 * P).rearrange("p (s g d) -> p s g d", s=2, g=NKV)
                act.activation(qk[:, 4, :, :], src[:, 0, :, :], ACT.Copy)
                act.activation(v_tok[b][:, :, :], src[:, 1, :, :], ACT.Copy).then_inc(in_out[b], 1)

            def take_z(d, c):
                used(d, c)
                if d > 0:
                    act.wait_ge(spat_ready, d)
                act.activation((gu if c == ZU else gv)[:, :], bank(IN_BANK[d, c]), ACT.Gelu)\
                    .then_inc(in_out[d % BLOCKS], 1)

            def take_gates(d, chunks):
                if d > 0:
                    act.wait_ge(mergedT_ps, d)
                for c in chunks:
                    used(d, c)
                    k = c - GA0
                    act.activation(sig[:, k // 2, (k % 2) * BANK:(k % 2 + 1) * BANK], bank(IN_BANK[d, c]), ACT.Sigmoid)\
                        .then_inc(in_out[d % BLOCKS], 1)

            def take_qkT(d):
                b = d % BLOCKS
                act.wait_ge(qkT_ps, d + 1)
                act.activation(qT[:, :, :], bank(0).rearrange("p (t n) -> p t n", t=GRP), ACT.Copy)
                act.activation(kT[b][:, :], bank(1, P), ACT.Copy).then_inc(qkT_ready, 1)

            def exps(d):
                b = d % BLOCKS
                act.wait_ge(att_max, d + 1)
                act.activation(att_m[:, 1, :], att_m[:, 1, :], ACT.Exp)
                for hh in range(NH):
                    row = probs[:, hh, 1 - b:2, :].rearrange("p s k -> p (s k)")
                    last = act.activation(row, row, ACT.Exp, bias=att_m[:, 0, hh:hh + 1],
                                          accum_out=att_m[:, 2, hh:hh + 1])
                last.then_inc(att_exp, 1)

            def take_probsT(d):
                b = d % BLOCKS
                act.wait_ge(probsT_ps, d + 1)
                src = att_psum(b)
                dst = turned[:, :, :].rearrange("p (h s) k -> p h s k", s=2)[:, :, 1 - b:2, :]
                for n in range(4):
                    last = act.activation(dst[:, 2 * n:2 * n + 2, :, :], src[:, 2 * n:2 * n + 2, :, :], ACT.Copy)
                last.then_inc(probsT_ready, 1)

            def take_spatT(d):
                act.wait_ge(branchT_ps, 2 * d + 1)
                act.activation(spatT[:, :, :], bank(1).rearrange("p (t n) -> p t n", t=4), ACT.Copy)\
                    .then_inc(branchT_ready, 1)

            def take_attnT(d):
                act.wait_ge(branchT_ps, 2 * d + 2)
                act.activation(attnT[:, :, :], bank(0).rearrange("p (t n) -> p t n", t=4), ACT.Copy)\
                    .then_inc(branchT_ready, 1)

            def take_mergedT(d):
                act.wait_ge(mergedT_ps, d + 1)
                act.activation(xT[d % BLOCKS][:, :, :], ps[:, 0:DM].rearrange("p (k n) -> p k n", k=KT), ACT.Copy)\
                    .then_inc(mergedT_ready, 1)

            def take_keysT(d):
                for half in range(2):
                    act.wait_ge(w_used, halves_used(d, KEYS) - 1 + half)
                    act.activation(keysT[:, half * 8:half * 8 + 8, :],
                                   ps[:, 6 * BANK:8 * BANK].rearrange("p (s k) -> p s k", s=8), ACT.Copy)\
                        .then_inc(keysT_ready, 1)

            def take_xfT(d):
                act.wait_ge(xfT_ps, d + 1)
                act.activation(xT[d % BLOCKS][:, :, :], ps[:, 0:DM].rearrange("p (k n) -> p k n", k=KT), ACT.Copy)\
                    .then_inc(xfT_ready, 1)

            def take_query(d, c):
                used(d, W_QRY0 + c)
                act.activation(turned[:, 4 * c:4 * c + 4, :], bank(4 + c).rearrange("p (s n) -> p s n", s=4),
                               ACT.Copy).then_inc(qry_ready, 1)

            def take_sides(d, c):
                act.wait_ge(side_ps, ROUTES * d + c + 1)
                act.activation(side_scores[:, 4 * c:4 * c + 4, :], bank(c % 2).rearrange("p (s n) -> p s n", s=4),
                               ACT.Copy).then_inc(side_ready, 1)

            def gate_exps(d, r):
                act.wait_ge(gate_args, ROUTES * d + r + 1)
                pairs = pair_s[:, r * R_HEADS:(r + 1) * R_HEADS, :]
                act.activation(pairs, pairs, ACT.Exp).then_inc(gate_exp, 1)

            def gelus(e, first, last):
                with act.Fori(first, last) as w:
                    act.wait_ge(u_used, w * UNIT + (e * PICKS + UNIT))
                    act.activation(acts[:, bass.ds(w * UNIT, UNIT)], dots[:, bass.ds(w * UNIT, UNIT)], ACT.Gelu)\
                        .then_inc(gelu_done, 1)

            root()
            take_xm(0)
            root()
            act.wait_ge(rope_args, 1)
            act.activation(sin[:, :, :], ang[:, :, :], ACT.Sin)
            act.activation(cos[:, :, :], turn_n[:, :, :], ACT.Sin).then_inc(rope_tab, 1)
            take_q(0)
            take_kv(0)
            take_xm(1)
            take_z(0, ZU)
            take_z(0, ZV)
            root()
            take_qkT(0)
            take_w_spT(0)
            take_gates(0, (GA0, GA1))
            exps(0)
            take_gates(0, (GB0, GB1))
            take_probsT(0)
            take_q(1)
            take_kv(1)
            take_spatT(0)
            take_attnT(0)
            take_z(1, ZU)
            take_mergedT(0)
            take_z(1, ZV)
            root()
            take_keysT(0)
            take_xfT(0)
            take_query(0, 0)
            take_sides(0, 0)
            take_query(0, 1)
            take_query(0, 2)
            take_sides(0, 1)
            gate_exps(0, 0)
            take_query(0, 3)
            take_sides(0, 2)
            take_sides(0, 3)

            for e in range(STEPS - 1):
                d = e + 1
                if d == 1:
                    take_gates(1, (GA0, GA1, GB0, GB1))
                    gelus(0, 0, 2)
                    gate_exps(0, 1)
                    gelus(0, 2, 3)
                    root()
                    take_qkT(1)
                    gelus(0, 3, 5)
                    gate_exps(0, 2)
                    gelus(0, 5, 7)
                    exps(1)
                    gelus(0, 7, 8)
                else:
                    gelus(e, 0, 2)
                    root()
                    take_xm(d)
                    take_q(d)
                    take_kv(d)
                    gelus(e, 2, 4)
                    gate_exps(e, 2)
                    take_z(d, ZU)
                    take_z(d, ZV)
                    gelus(e, 4, 6)
                    gate_exps(e, 3)
                    take_gates(d, (GA0, GA1))
                    take_qkT(d)
                    take_gates(d, (GB0, GB1))
                    if d % BLOCKS == 0:
                        take_w_spT(d)
                    gelus(e, 6, 7)
                    root()
                    exps(d)
                    gelus(e, 7, 8)
                take_probsT(d)
                gelus(e, 8, 9)
                take_spatT(d)
                gelus(e, 9, 10)
                take_attnT(d)
                gelus(e, 10, 11)
                if d == 1:
                    gate_exps(0, 3)
                take_mergedT(d)
                gelus(e, 11, 12)
                if d % BLOCKS == 0:
                    take_keysT(d)
                root()
                take_xfT(d)
                take_query(d, 0)
                gelus(e, 12, 13)
                take_sides(d, 0)
                take_query(d, 1)
                for c in range(2, ROUTES):
                    take_query(d, c)
                    take_sides(d, c - 1)
                take_sides(d, ROUTES - 1)
                gelus(e, 13, 14)
                gate_exps(d, 0)
                gelus(e, 14, 16)
                gate_exps(d, 1)

            e = STEPS - 1
            gelus(e, 0, 5)
            gate_exps(e, 2)
            gelus(e, 5, 9)
            gate_exps(e, 3)
            gelus(e, 9, 12)
            root()
            gelus(e, 12, UNITS)
            root()

        @block_ctx.vector
        def _(vec):
            links = [0]

            def link(ins):
                links[0] += 1
                ins.then_inc(dve, 1)
                vec.wait_ge(dve, links[0])

            roots = [0]

            def rsqrt_of_stat():
                roots[0] += 1
                vec.wait_ge(sq_out, roots[0])
                link(vec.reciprocal(stat[:, 2:3], stat[:, 1:2]))
                link(vec.scalar_tensor_tensor(out=stat[:, 4:5], in0=stat[:, 2:3], scalar=stat[:, 2:3],
                                              in1=stat[:, 0:1], op0=ALU.mult, op1=ALU.mult))
                link(vec.tensor_scalar(stat[:, 4:5], stat[:, 4:5], -0.5, 1.5, ALU.mult, ALU.add))
                link(vec.tensor_tensor(stat[:, 3:4], stat[:, 2:3], stat[:, 4:5], ALU.mult))

            def mean_square(src, spare, width):
                link(vec.scalar_tensor_tensor(out=spare, in0=src, scalar=1.0, in1=src, op0=ALU.mult, op1=ALU.mult,
                                              accum_out=stat[:, 5:6]))
                vec.tensor_scalar(stat[:, 0:1], stat[:, 5:6], 1.0 / width, EPS, ALU.mult, ALU.add).then_inc(sq_in, 1)

            def norm_begin(src):
                mean_square(src[:, :], junk[:, :], DM)

            def norm_end(src, dst, gain, ready):
                rsqrt_of_stat()
                vec.scalar_tensor_tensor(out=dst[:, :], in0=src[:, :], scalar=stat[:, 3:4], in1=gain[:, :],
                                         op0=ALU.mult, op1=ALU.mult).then_inc(ready, 1)

            def rope_tables():
                vec.memset(w_spT[CH:P, :, 0:CH], 0.0)
                for j in range(HALF):
                    last = vec.memset(inv_freq[:, j:j + 1], float(np.float32(THETA ** (-j / HALF))))
                link(last)
                for b in range(BLOCKS):
                    link(vec.tensor_copy(stat[:, 6:7], pos[:, b:b + 1]))
                    link(vec.tensor_scalar(ang[:, b, :], inv_freq[:, :], stat[:, 6:7], None, ALU.mult))
                link(vec.tensor_scalar(turn_n[:, :, :], ang[:, :, :], float(1 / (2 * np.pi)), ROUND, ALU.mult, ALU.add))
                link(vec.tensor_scalar(turn_n[:, :, :], turn_n[:, :, :], -ROUND, None, ALU.add))
                for part in two_pi_parts():
                    link(vec.scalar_tensor_tensor(out=ang[:, :, :], in0=turn_n[:, :, :], scalar=-part,
                                                  in1=ang[:, :, :], op0=ALU.mult, op1=ALU.add))
                link(vec.tensor_scalar(ang[:, :, :], ang[:, :, :], PI_DOWN, -PI_DOWN, ALU.min, ALU.max))
                link(vec.tensor_scalar(turn_n[:, :, :], ang[:, :, :], -1.0, None, ALU.mult))
                link(vec.tensor_tensor(turn_n[:, :, :], turn_n[:, :, :], ang[:, :, :], ALU.min))
                vec.tensor_scalar(turn_n[:, :, :], turn_n[:, :, :], float(np.pi / 2), None, ALU.add)\
                    .then_inc(rope_args, 1)

            def rope(d):
                b = d % BLOCKS
                vec.wait_ge(in_out[b], 8 * (d // BLOCKS) + KV + 1)
                if d == 0:
                    vec.wait_ge(rope_tab, 1)
                heads = qk[:, :, :, :].rearrange("p t g d -> p (t g) d")
                lo, hi = heads[:, :, 0:HALF], heads[:, :, HALF:ROT]
                c = cos[:, b, :].unsqueeze(1).to_broadcast([P, 10, HALF])
                s = sin[:, b, :].unsqueeze(1).to_broadcast([P, 10, HALF])
                vec.tensor_tensor(rt[:, 0], lo, c, ALU.mult)
                vec.tensor_tensor(rt[:, 1], hi, s, ALU.mult)
                vec.tensor_tensor(rt[:, 2], hi, c, ALU.mult)
                link(vec.tensor_tensor(rt[:, 3], lo, s, ALU.mult))
                vec.tensor_tensor(lo, rt[:, 0], rt[:, 1], ALU.subtract)
                vec.tensor_tensor(hi, rt[:, 2], rt[:, 3], ALU.add).then_inc(roped, 1)

            def layer_norm_begin(d):
                vec.wait_ge(in_out[d % BLOCKS], 8 * (d // BLOCKS) + ZV + 1)
                if d % BLOCKS == 0:
                    vec.wait_ge(gains_in, 16 * 4 * (d // BLOCKS + 1))
                link(vec.reduce_sum(stat[:, 6:7], gv[:, :], AX))
                link(vec.tensor_scalar(stat[:, 6:7], stat[:, 6:7], -1.0 / GW, None, ALU.mult))
                link(vec.tensor_scalar(gv[:, :], gv[:, :], stat[:, 6:7], None, ALU.add))
                mean_square(gv[:, :], spat[:, :], GW)

            def layer_norm_end(d):
                rsqrt_of_stat()
                link(vec.scalar_tensor_tensor(out=gv[:, :], in0=gv[:, :], scalar=stat[:, 3:4], in1=ln_g[:, :],
                                              op0=ALU.mult, op1=ALU.mult))
                vec.tensor_tensor(gv[:, :], gv[:, :], ln_b[:, :], ALU.add).then_inc(ln_ready, 1)

            def softmax_args(d):
                l, b = divmod(d, BLOCKS)
                if d == 0:
                    vec.wait_ge(consts, 7)
                    vec.wait_ge(small_in, 16 * 3)
                vec.wait_ge(att_ps, d + 1)
                cols = (1 + b) * P
                src = att_psum(b).rearrange("p h s k -> p h (s k)")
                dst = probs[:, :, :, :].rearrange("p h s k -> p h (s k)")[:, :, 2 * P - cols:2 * P]
                m = mask[:, :, :].rearrange("p s k -> p (s k)")[:, 2 * P - cols:2 * P]
                m = m.unsqueeze(1).to_broadcast([P, NH, cols])
                link(vec.scalar_tensor_tensor(out=dst, in0=src, scalar=float(HD ** -0.5), in1=m,
                                              op0=ALU.mult, op1=ALU.add))
                link(vec.tensor_reduce(att_m[:, 0, :], dst, AX, ALU.max))
                link(vec.tensor_tensor(att_m[:, 0, :], att_m[:, 0, :], sinks[:, l, :], ALU.max))
                link(vec.tensor_tensor(att_m[:, 1, :], sinks[:, l, :], att_m[:, 0, :], ALU.subtract))
                vec.tensor_scalar(att_m[:, 0, :], att_m[:, 0, :], -1.0, None, ALU.mult).then_inc(att_max, 1)

            def spatial_gate(d):
                l = d // BLOCKS
                vec.wait_ge(spat_ps, d + 1)
                for g in range(GG):
                    last = vec.scalar_tensor_tensor(
                        out=spat[:, g * GD:(g + 1) * GD], in0=ps[:, BANK + g * GD:BANK + (g + 1) * GD],
                        scalar=b_sp[:, l, g:g + 1], in1=gu[:, g * GD:(g + 1) * GD], op0=ALU.add, op1=ALU.mult)
                last.then_inc(spat_ready, 1)

            def attention_out(d):
                vec.wait_ge(pv_ps, d + 1)
                link(vec.tensor_tensor(att_m[:, 3, :], att_m[:, 2, :], att_m[:, 1, :], ALU.add))
                link(vec.reciprocal(att_m[:, 3, :], att_m[:, 3, :]))
                vec.tensor_tensor(attn[:, :, :], bank(0).rearrange("p (h d) -> p h d", h=NH),
                                  att_m[:, 3, :].unsqueeze(2).to_broadcast([P, NH, HD]), ALU.mult)\
                    .then_inc(attn_ready, 1)

            def merge(d):
                vec.wait_ge(w_used, halves_used(d, W_ATTN))
                vec.tensor_tensor(sig[:, 0, :], sig[:, 0, :], ps[:, 4 * BANK:6 * BANK], ALU.mult)
                link(vec.tensor_tensor(sig[:, 1, :], sig[:, 1, :], ps[:, 6 * BANK:8 * BANK], ALU.mult))
                vec.tensor_tensor(sig[:, 0, :], sig[:, 0, :], sig[:, 1, :], ALU.add).then_inc(merged, 1)

            def add_mixer(d):
                b = d % BLOCKS
                vec.wait_ge(w_used, halves_used(d, W_OUT1))
                link(vec.tensor_tensor(h[b][:, :], h[b][:, :], ps[:, 4 * BANK:6 * BANK], ALU.add))
                norm_begin(h[b])
                norm_end(h[b], xf[b], gain_ffn, xf_ready)

            def top16(scores, values, indices):
                link(vec.max(values[:, 0:8], scores))
                vec.max_index(indices[:, 0:8], values[:, 0:8], scores)
                link(vec.match_replace(scores, values[:, 0:8], scores, LOWEST))
                link(vec.max(values[:, 8:16], scores))
                return vec.max_index(indices[:, 8:16], values[:, 8:16], scores)

            def side_top(d, r, parts=slice(0, R_HEADS)):
                vec.wait_ge(side_ready, ROUTES * d + r + 1)
                for s in range(r * R_SIDES + 2 * parts.start, r * R_SIDES + 2 * parts.stop):
                    last = top16(side_scores[:, s, :], top_v[:, s, :], top_i[:, s, :])
                link(last)

            def experts(d, r, parts=slice(0, R_HEADS)):
                l, n = d // BLOCKS, parts.stop - parts.start
                heads = slice(r * R_HEADS + parts.start, r * R_HEADS + parts.stop)
                picks = slice(heads.start * TOPK, heads.stop * TOPK)
                for hh in range(heads.start, heads.stop):
                    c = cand[:, hh % 2, :, :]
                    link(vec.tensor_tensor(c, top_v[:, 2 * hh, :].unsqueeze(2).to_broadcast([P, TOPK, TOPK]),
                                           top_v[:, 2 * hh + 1, :].unsqueeze(1).to_broadcast([P, TOPK, TOPK]), ALU.add))
                    last = top16(c.rearrange("p a b -> p (a b)"), pair_s[:, hh, :],
                                 pair_i[:, hh * TOPK:(hh + 1) * TOPK])
                link(last)
                link(vec.tensor_copy(gsum[:, heads], pair_s[:, heads, 0]))
                last = vec.tensor_tensor(pair_s[:, heads, :], pair_s[:, heads, :],
                                         gsum[:, heads].unsqueeze(2).to_broadcast([P, n, TOPK]), ALU.subtract)
                if parts.stop == R_HEADS:
                    last.then_inc(gate_args, 1)
                vec.tensor_single_scalar(pair_ab[:, 0, picks], pair_i[:, picks], 4, ALU.logical_shift_right)
                link(vec.tensor_single_scalar(pair_ab[:, 1, picks], pair_i[:, picks], TOPK - 1, ALU.bitwise_and))
                for side in range(2):
                    last = vec.tensor_tensor(one_hot[:, side, 0:n * TOPK, :],
                                             pair_ab[:, side, picks].unsqueeze(2).to_broadcast([P, n * TOPK, TOPK]),
                                             iota[:, :].unsqueeze(1).to_broadcast([P, n * TOPK, TOPK]), ALU.is_equal)
                link(last)
                for side in range(2):
                    per_head = one_hot[:, side, 0:n * TOPK, :].rearrange("p (h j) m -> p h j m", h=n)
                    places = top_i[:, :, :].rearrange("p (h t) m -> p h t m", t=2)[:, heads, side, :]
                    last = vec.tensor_tensor(per_head, per_head,
                                             places.unsqueeze(2).to_broadcast([P, n, TOPK, TOPK]), ALU.mult)
                link(last)
                link(vec.tensor_reduce(key_ab[:, 0:2, picks], one_hot[:, :, 0:n * TOPK, :], AX, ALU.add))
                link(vec.scalar_tensor_tensor(out=key_ab[:, 2, picks], in0=key_ab[:, 0, picks], scalar=float(NK),
                                              in1=key_ab[:, 1, picks], op0=ALU.mult, op1=ALU.add))
                vec.tensor_scalar(ids[:, d * PICKS + picks.start:d * PICKS + picks.stop], key_ab[:, 2, picks],
                                  float(l * NE), None, ALU.add).then_inc(routed, 1)

            def gate(d, r):
                heads = slice(r * R_HEADS, (r + 1) * R_HEADS)
                picks = slice(r * R_PICKS, (r + 1) * R_PICKS)
                vec.wait_ge(gate_exp, ROUTES * d + r + 1)
                link(vec.reduce_sum(gsum[:, heads], pair_s[:, heads, :], AX))
                link(vec.reciprocal(gsum[:, heads], gsum[:, heads]))
                vec.tensor_tensor(gates[d % BLOCKS][:, picks].rearrange("p (h j) -> p h j", h=R_HEADS), pair_s[:, heads, :],
                                  gsum[:, heads].unsqueeze(2).to_broadcast([P, R_HEADS, TOPK]), ALU.mult)\
                    .then_inc(routed, 1)

            def route(d, r):
                experts(d, r)
                gate(d, r)

            def u_pick(e, w, i):
                vec.wait_ge(u_landed[i % RING], w * (16 * TURNS) + 16 * (e * UNITS * TURNS + i // RING + 1))
                vec.scalar_tensor_tensor(out=junk[:, :], in0=xf[e % BLOCKS][:, :], scalar=1.0,
                                         in1=u_ring[:, i % RING, :], op0=ALU.mult, op1=ALU.mult,
                                         accum_out=dots[:, bass.ds(w * UNIT + i, 1)]).then_inc(u_used, 1)

            def coefficients(e, w, ve, vw):
                cols = bass.ds(vw * UNIT, UNIT)
                vec.wait_ge(gelu_done, w + (e * UNITS - LAG + 1))
                vec.tensor_tensor(coef[:, cols], acts[:, cols], gates[ve % BLOCKS][:, cols], ALU.mult)\
                    .then_inc(coef_ready, 1)
                vec.wait_ge(coef_ready, w + (e * UNITS - LAG + 1))

            def v_pick(e, w, ve, vw, i):
                hb = h[ve % BLOCKS]
                vec.wait_ge(v_landed[i % RING], w * (16 * TURNS) + 16 * ((e * UNITS - LAG) * TURNS + i // RING + 1))
                vec.scalar_tensor_tensor(out=hb[:, :], in0=v_ring[:, i % RING, :],
                                         scalar=coef[:, bass.ds(vw * UNIT + i, 1)],
                                         in1=hb[:, :], op0=ALU.mult, op1=ALU.add).then_inc(v_used, 1)

            def units(e, first, last):
                before = first < LAG
                assert before == (last <= LAG)
                has_u, has_v = e < STEPS, e > 0 or not before
                with vec.Fori(first, last) as w:
                    ve, vw = (e - 1, w + (UNITS - LAG)) if before else (e, w - LAG)
                    if has_v:
                        coefficients(e, w, ve, vw)
                    for i in range(UNIT):
                        if has_u:
                            u_pick(e, w, i)
                        if has_v:
                            if i > 0:
                                vec.wait_ge(v_used, w * UNIT + (e * PICKS - LAG * UNIT + i))
                            v_pick(e, w, ve, vw, i)
                        if has_u:
                            vec.wait_ge(u_used, w * UNIT + (e * PICKS + i + 1))
                    if has_v:
                        vec.wait_ge(v_used, w * UNIT + (e * PICKS - LAG * UNIT + UNIT))

            vec.wait_ge(x0_in, 16 * 2)
            norm_begin(h[0])
            vec.wait_ge(mix_in, 16)
            norm_end(h[0], xf[0], gain_mix, xm_ready)
            vec.wait_ge(x1_in, 16)
            norm_begin(h[1])
            norm_end(h[1], xf[1], gain_mix, xm_ready)
            rope_tables()
            rope(0)
            layer_norm_begin(0)
            layer_norm_end(0)
            softmax_args(0)
            spatial_gate(0)
            attention_out(0)
            merge(0)
            add_mixer(0)
            for head in range(R_HEADS):
                side_top(0, 0, slice(head, head + 1))
                experts(0, 0, slice(head, head + 1))
            gate(0, 0)

            units(0, 0, 1)
            side_top(0, 1)
            units(0, 1, 2)
            route(0, 1)
            units(0, 2, 3)
            rope(1)
            layer_norm_begin(1)
            layer_norm_end(1)
            units(0, 3, 4)
            side_top(0, 2)
            units(0, 4, 5)
            route(0, 2)
            units(0, 5, 7)
            side_top(0, 3)
            softmax_args(1)
            units(0, 7, 8)
            spatial_gate(1)
            units(0, 8, 9)
            attention_out(1)
            units(0, 9, 10)
            merge(1)
            units(0, 10, 11)
            route(0, 3)
            units(0, 11, 12)
            add_mixer(1)
            units(0, 12, 13)
            side_top(1, 0)
            units(0, 13, 14)
            route(1, 0)
            units(0, 14, 15)
            side_top(1, 1)
            units(0, 15, UNITS)
            route(1, 1)
            for e in range(1, STEPS - 1):
                d, b = e + 1, (e + 1) % BLOCKS
                units(e, 0, 2)
                norm_begin(h[b])
                vec.wait_ge(mix_in, 16 * 2)
                norm_end(h[b], xf[b], gain_mix, xm_ready)
                units(e, 2, 3)
                side_top(e, 2)
                units(e, 3, 4)
                route(e, 2)
                units(e, 4, 5)
                side_top(e, 3)
                units(e, 5, 6)
                route(e, 3)
                rope(d)
                units(e, 6, 7)
                layer_norm_begin(d)
                layer_norm_end(d)
                softmax_args(d)
                units(e, 7, 8)
                spatial_gate(d)
                units(e, 8, 9)
                attention_out(d)
                units(e, 9, 10)
                merge(d)
                units(e, 10, 12)
                add_mixer(d)
                units(e, 12, 13)
                side_top(d, 0)
                units(e, 13, 14)
                route(d, 0)
                units(e, 14, 15)
                side_top(d, 1)
                units(e, 15, UNITS)
                route(d, 1)

            e = STEPS - 1
            units(e, 0, 2)
            units(e, 2, 3)
            side_top(e, 2)
            units(e, 3, 5)
            route(e, 2)
            units(e, 5, 7)
            side_top(e, 3)
            units(e, 7, 9)
            route(e, 3)
            units(e, 9, 12)
            norm_begin(h[0])
            vec.wait_ge(mix_in, 16 * 3)
            norm_end(h[0], xf[0], gain_mix, y_ready)
            units(e, 12, UNITS)
            units(STEPS, 0, LAG)
            norm_begin(h[1])
            norm_end(h[1], xf[1], gain_mix, y_ready)


_INS = ["x", "positions", "norm_mix_g", "w_in", "attn_sinks", "gmlp_ln_g", "gmlp_ln_b", "w_spatial", "b_spatial",
        "w_attn_branch", "w_gmlp_branch", "w_out", "norm_ffn_g", "peer_w_query", "peer_sub_keys", "peer_u", "peer_v",
        "final_norm_g"]


def kernel(**inputs):
    import concourse.bacc as _bacc
    from concourse.bass_utils import run_bass_kernel_spmd as _run

    nc = _bacc.Bacc("TRN2", target_bir_lowering=False, num_devices=1)
    arrays, args = {}, []
    for name in _INS:
        a = np.ascontiguousarray(inputs[name])
        arrays[f"in_{name}"] = a
        args.append(nc.dram_tensor(f"in_{name}", a.shape, mybir.dt.from_np(a.dtype), kind="ExternalInput").ap())
    args.append(nc.dram_tensor("out_trunk", (1, BLOCKS * P, DM), F32, kind="ExternalOutput").ap())
    build(nc, *args)
    r = _run(nc, [arrays], core_ids=[0])
    return r.results[0]["out_trunk"]
```
